# Optimizing a Trainium2 kernel written in Bass

```python
import jax, jax.numpy as jnp
from jax import lax
import numpy as np
import math

D_MODEL = 1024
BATCH = 1
SEQ = 512
DEPTH = 1

HEAD_DIM = 64
A_HEADS = 8
A_Q_RANK = 256
A_V_LATENT = 128
IDX_HEADS = 8
IDX_DIM = 64
B_HEADS = 8
D_FF = 2816
MAX_TOPK = 256
Q_BLOCK = 128
ROPE_THETA = 10000.0
EPS = 1e-6
A_WIDTH = A_HEADS * HEAD_DIM
B_WIDTH = B_HEADS * HEAD_DIM
IN_SPLITS = (A_Q_RANK, HEAD_DIM, A_V_LATENT, IDX_DIM, IDX_HEADS,
             B_WIDTH, B_WIDTH, B_WIDTH, D_MODEL, D_MODEL)
IN_COLS = sum(IN_SPLITS)


def rms_norm(x, g):
    xf = x.astype(jnp.float32)
    y = xf * lax.rsqrt(jnp.mean(xf * xf, axis=-1, keepdims=True) + EPS)
    return (y * g.astype(jnp.float32)).astype(x.dtype)

def swiglu(h, w_gate, w_up, w_down):
    return (jax.nn.silu(h @ w_gate) * (h @ w_up)) @ w_down

def rope_tables(positions, dim):
    inv_freq = ROPE_THETA ** (-jnp.arange(0, dim, 2, dtype=jnp.float32) / dim)
    ang = positions.astype(jnp.float32)[..., None] * inv_freq
    return jnp.cos(ang), jnp.sin(ang)

def apply_rope(x, cos, sin):
    xf = x.astype(jnp.float32)
    x1, x2 = jnp.split(xf, 2, axis=-1)
    return jnp.concatenate([x1 * cos - x2 * sin, x1 * sin + x2 * cos], axis=-1).astype(x.dtype)

def dsa_attention(q_a, k_a, v_a, q_idx, k_idx, w_idx, w_uv, top_k):
    bsz, seq = k_a.shape[0], k_a.shape[1]
    n_blocks = seq // Q_BLOCK
    key_pos = jnp.arange(seq)

    def block(i):
        q0 = i * Q_BLOCK
        qa = lax.dynamic_slice_in_dim(q_a, q0, Q_BLOCK, axis=1)
        qi = lax.dynamic_slice_in_dim(q_idx, q0, Q_BLOCK, axis=1)
        wi = lax.dynamic_slice_in_dim(w_idx, q0, Q_BLOCK, axis=1)
        t_pos = q0 + jnp.arange(Q_BLOCK)
        dots = jnp.einsum('bthd,bsd->bths', qi.astype(jnp.float32), k_idx.astype(jnp.float32))
        score = jnp.einsum('bths,bth->bts', jax.nn.relu(dots), wi.astype(jnp.float32))
        causal = key_pos[None, :] <= t_pos[:, None]
        score = jnp.where(causal[None], score, -jnp.inf)
        _, idx = lax.top_k(score, top_k)
        valid = idx <= t_pos[None, :, None]
        flat = idx.reshape(bsz, Q_BLOCK * top_k)[:, :, None]
        kg = jnp.take_along_axis(k_a, flat, axis=1).reshape(bsz, Q_BLOCK, top_k, HEAD_DIM)
        vg = jnp.take_along_axis(v_a, flat, axis=1).reshape(bsz, Q_BLOCK, top_k, A_V_LATENT)
        logits = jnp.einsum('bthd,btkd->bthk', qa.astype(jnp.float32), kg.astype(jnp.float32)) * (HEAD_DIM ** -0.5)
        logits = jnp.where(valid[:, :, None, :], logits, -jnp.inf)
        p = jax.nn.softmax(logits, axis=-1).astype(v_a.dtype)
        o_lat = jnp.einsum('bthk,btkc->bthc', p, vg)
        o = jnp.einsum('bthc,hcd->bthd', o_lat, w_uv)
        return o.reshape(bsz, Q_BLOCK, A_WIDTH)

    out = lax.map(block, jnp.arange(n_blocks))
    return out.transpose(1, 0, 2, 3).reshape(bsz, seq, A_WIDTH)

def stick_breaking_attention(q_b, k_b, v_b):
    bsz, seq = q_b.shape[0], q_b.shape[1]
    n_blocks = seq // Q_BLOCK
    key_pos = jnp.arange(seq)

    def block(i):
        q0 = i * Q_BLOCK
        qb = lax.dynamic_slice_in_dim(q_b, q0, Q_BLOCK, axis=1)
        t_pos = q0 + jnp.arange(Q_BLOCK)
        z = jnp.einsum('bthd,bshd->bhts', qb.astype(jnp.float32), k_b.astype(jnp.float32)) * (HEAD_DIM ** -0.5)
        strict = (key_pos[None, :] < t_pos[:, None])[None, None]
        log_not = jnp.where(strict, jax.nn.log_sigmoid(-z), 0.0)
        between = lax.cumsum(log_not, axis=3, reverse=True) - log_not
        log_a = jax.nn.log_sigmoid(z) + between
        a = jnp.where(strict, jnp.exp(log_a), 0.0).astype(v_b.dtype)
        o = jnp.einsum('bhts,bshd->bthd', a, v_b)
        return o.reshape(bsz, Q_BLOCK, B_WIDTH)

    out = lax.map(block, jnp.arange(n_blocks))
    return out.transpose(1, 0, 2, 3).reshape(bsz, seq, B_WIDTH)

def first_inputs(seed: int = 0) -> dict:
    key = jax.random.key(seed)
    ks = jax.random.split(key, 24)
    f32 = jnp.float32

    def w(k, shape, fan_in):
        return jax.random.normal(k, shape, f32) * (fan_in ** -0.5)

    def gain(k, shape):
        return 1.0 + 0.02 * jax.random.normal(k, shape, f32)

    L = DEPTH
    return {
        'x': jax.random.normal(ks[0], (BATCH, SEQ, D_MODEL), f32),
        'positions': jnp.broadcast_to(jnp.arange(SEQ, dtype=jnp.int32), (BATCH, SEQ)),
        'g_ffn1': gain(ks[1], (L, D_MODEL)),
        'w1_gate': w(ks[2], (L, D_MODEL, D_FF), D_MODEL),
        'w1_up': w(ks[3], (L, D_MODEL, D_FF), D_MODEL),
        'w1_down': w(ks[4], (L, D_FF, D_MODEL), D_FF),
        'g_mix': gain(ks[5], (L, D_MODEL)),
        'w_in': w(ks[6], (L, D_MODEL, IN_COLS), D_MODEL),
        'g_cq': gain(ks[7], (L, A_Q_RANK)),
        'w_uq_a': w(ks[8], (L, A_Q_RANK, A_WIDTH), A_Q_RANK),
        'w_q_idx': w(ks[9], (L, A_Q_RANK, IDX_HEADS * IDX_DIM), A_Q_RANK),
        'g_q_a': gain(ks[10], (L, HEAD_DIM)),
        'g_k_a': gain(ks[11], (L, HEAD_DIM)),
        'w_uv_a': w(ks[12], (L, A_HEADS, A_V_LATENT, HEAD_DIM), A_V_LATENT),
        'w_o_a': w(ks[13], (L, A_WIDTH, D_MODEL), A_WIDTH),
        'w_o_b': w(ks[14], (L, B_WIDTH, D_MODEL), B_WIDTH),
        'w_out': w(ks[15], (L, D_MODEL, D_MODEL), D_MODEL),
        'g_ffn2': gain(ks[16], (L, D_MODEL)),
        'w2_gate': w(ks[17], (L, D_MODEL, D_FF), D_MODEL),
        'w2_up': w(ks[18], (L, D_MODEL, D_FF), D_MODEL),
        'w2_down': w(ks[19], (L, D_FF, D_MODEL), D_FF),
    }

def first_block(x, positions, g_ffn1, w1_gate, w1_up, w1_down, g_mix, w_in, g_cq, w_uq_a, w_q_idx,
              g_q_a, g_k_a, w_uv_a, w_o_a, w_o_b, w_out, g_ffn2, w2_gate, w2_up, w2_down):
    bsz, seq, _ = x.shape
    top_k = min(MAX_TOPK, seq // 4)
    cos, sin = rope_tables(positions, HEAD_DIM)
    cos_h, sin_h = cos[:, :, None, :], sin[:, :, None, :]
    offsets = [int(o) for o in np.cumsum(IN_SPLITS)[:-1]]
    for l in range(DEPTH):
        x = x + 0.5 * swiglu(rms_norm(x, g_ffn1[l]), w1_gate[l], w1_up[l], w1_down[l])

        h = rms_norm(x, g_mix[l])
        proj = h @ w_in[l]
        (c_q, k_a, v_a, k_idx, w_idx, q_b, k_b, v_b, gate_a, gate_b) = jnp.split(proj, offsets, axis=-1)

        c_q = rms_norm(c_q, g_cq[l])
        q_a = (c_q @ w_uq_a[l]).reshape(bsz, seq, A_HEADS, HEAD_DIM)
        q_a = apply_rope(rms_norm(q_a, g_q_a[l]), cos_h, sin_h)
        k_a = apply_rope(rms_norm(k_a, g_k_a[l]), cos, sin)
        q_idx = apply_rope((c_q @ w_q_idx[l]).reshape(bsz, seq, IDX_HEADS, IDX_DIM), cos_h, sin_h)
        k_idx = apply_rope(k_idx, cos, sin)
        w_idx = w_idx * ((IDX_HEADS ** -0.5) * (IDX_DIM ** -0.5))
        y_a = dsa_attention(q_a, k_a, v_a, q_idx, k_idx, w_idx, w_uv_a[l], top_k)

        y_b = stick_breaking_attention(q_b.reshape(bsz, seq, B_HEADS, HEAD_DIM),
                                       k_b.reshape(bsz, seq, B_HEADS, HEAD_DIM),
                                       v_b.reshape(bsz, seq, B_HEADS, HEAD_DIM))

        merged = jax.nn.sigmoid(gate_a) * (y_a @ w_o_a[l]) + jax.nn.sigmoid(gate_b) * (y_b @ w_o_b[l])
        x = x + merged @ w_out[l]

        x = x + 0.5 * swiglu(rms_norm(x, g_ffn2[l]), w2_gate[l], w2_up[l], w2_down[l])
    return x


CHUNK = 64
D_MIX = D_MODEL
M_HEADS = 4
M_WIDTH = D_MIX // 2
M_HEAD_DIM = M_WIDTH // M_HEADS
CONV_WIDTH = 4
A_HEADS_2 = 4
A_WIDTH_2 = D_MIX - M_WIDTH
A_HEAD_DIM = A_WIDTH_2 // A_HEADS_2
A_QK_DIM = A_HEAD_DIM // 2
IN_SIZES = (2 * M_WIDTH, M_WIDTH, M_WIDTH, M_HEADS, M_HEADS, A_WIDTH_2, A_WIDTH_2, A_WIDTH_2)
IN_COLS_2 = sum(IN_SIZES)
IN_SPLITS_2 = tuple(int(s) for s in np.cumsum(IN_SIZES)[:-1])
N_GROUPS = 4
EXPERTS_PER_GROUP = 8
N_EXPERTS = N_GROUPS * EXPERTS_PER_GROUP
TOP_K = 2
D_EXPERT = D_MODEL // 2
MOE_BLOCK = 256


def rms_norm_2(x, w):
    xf = x.astype(jnp.float32)
    y = xf * lax.rsqrt(jnp.mean(xf * xf, axis=-1, keepdims=True) + EPS)
    return (y * w.astype(jnp.float32)).astype(x.dtype)

def causal_conv(x, w, b):
    S = x.shape[1]
    xp = jnp.pad(x, ((0, 0), (CONV_WIDTH - 1, 0), (0, 0)))
    out = b
    for j in range(CONV_WIDTH):
        out = out + xp[:, j:j + S] * w[j]
    return out

def mlstm_chunkwise(q, k, v, i_pre, f_pre):
    Bn, S, H, Dh = q.shape
    NC = S // CHUNK

    def to_chunks(t):
        t = t.astype(jnp.float32).reshape((Bn, NC, CHUNK) + t.shape[2:])
        return jnp.moveaxis(jnp.moveaxis(t, 1, 0), 3, 2)

    qc = to_chunks(q)
    kc = to_chunks(k) * (Dh ** -0.5)
    vc = to_chunks(v)
    ic = to_chunks(i_pre)
    fc = jax.nn.log_sigmoid(to_chunks(f_pre))
    causal = jnp.tril(jnp.ones((CHUNK, CHUNK), dtype=bool))

    def step(carry, inp):
        C, n, m = carry
        q_c, k_c, v_c, i_c, lf_c = inp
        b = jnp.cumsum(lf_c, axis=-1)
        log_d = jnp.where(causal, b[..., :, None] - b[..., None, :] + i_c[..., None, :], -jnp.inf)
        log_inter = b + m[..., None]
        m_t = jnp.maximum(log_inter, jnp.max(log_d, axis=-1))
        d = jnp.exp(log_d - m_t[..., None])
        inter = jnp.exp(log_inter - m_t)
        s = jnp.einsum('bhtd,bhsd->bhts', q_c, k_c) * d
        num = jnp.einsum('bhts,bhse->bhte', s, v_c) + inter[..., None] * jnp.einsum('bhtd,bhde->bhte', q_c, C)
        den = jnp.sum(s, axis=-1) + inter * jnp.einsum('bhtd,bhd->bht', q_c, n)
        h = num / jnp.maximum(jnp.abs(den), jnp.exp(-m_t))[..., None]
        b_end = b[..., -1]
        log_w = b_end[..., None] - b + i_c
        m_new = jnp.maximum(b_end + m, jnp.max(log_w, axis=-1))
        w = jnp.exp(log_w - m_new[..., None])
        decay = jnp.exp(b_end + m - m_new)
        C_new = decay[..., None, None] * C + jnp.einsum('bhs,bhsd,bhse->bhde', w, k_c, v_c)
        n_new = decay[..., None] * n + jnp.einsum('bhs,bhsd->bhd', w, k_c)
        return (C_new, n_new, m_new), h

    init = (jnp.zeros((Bn, H, Dh, Dh), jnp.float32),
            jnp.zeros((Bn, H, Dh), jnp.float32),
            jnp.zeros((Bn, H), jnp.float32))
    _, h = lax.scan(step, init, (qc, kc, vc, ic, fc))
    h = jnp.moveaxis(jnp.moveaxis(h, 0, 1), 2, 3)
    return h.reshape(Bn, S, H, Dh)

def diff_attention(q, k, v, q_norm_w, k_norm_w, lq1, lk1, lq2, lk2, a_norm_w, lambda_init):
    Bn, S = q.shape[:2]
    NQ = S // Q_BLOCK
    q = rms_norm_2(q, q_norm_w)
    k = rms_norm_2(k, k_norm_w)
    f32 = jnp.float32
    lam = (jnp.exp(jnp.sum(lq1.astype(f32) * lk1.astype(f32)))
           - jnp.exp(jnp.sum(lq2.astype(f32) * lk2.astype(f32))) + lambda_init)
    kt = jnp.transpose(k, (0, 2, 3, 1, 4))
    vt = jnp.transpose(v, (0, 2, 1, 3))
    qb = q.reshape(Bn, NQ, Q_BLOCK, A_HEADS_2, 2, A_QK_DIM).transpose(1, 0, 3, 4, 2, 5)
    key_chunk = jnp.arange(S) // CHUNK
    scale = A_QK_DIM ** -0.5

    def block(args):
        q_blk, idx = args
        q_chunk = (idx * Q_BLOCK + jnp.arange(Q_BLOCK)) // CHUNK
        mask = key_chunk[None, :] <= q_chunk[:, None]
        s = jnp.einsum('bhcqd,bhcsd->bhcqs', q_blk, kt).astype(f32) * scale
        p = jax.nn.softmax(jnp.where(mask, s, -jnp.inf), axis=-1)
        attn = p[:, :, 0] - lam * p[:, :, 1]
        return jnp.einsum('bhqs,bhsd->bhqd', attn.astype(v.dtype), vt)

    o = lax.map(block, (qb, jnp.arange(NQ)))
    o = o.transpose(1, 0, 3, 2, 4).reshape(Bn, S, A_HEADS_2, A_HEAD_DIM)
    o = rms_norm_2(o, a_norm_w) * (1.0 - lambda_init)
    return o.reshape(Bn, S, A_WIDTH_2)

def hybrid_mixer(h, w_in, b_igate, b_fgate, conv_w, conv_b, m_norm_w, q_norm_w, k_norm_w,
                 lq1, lk1, lq2, lk2, a_norm_w, w_out, lambda_init):
    Bn, S, _ = h.shape
    proj = h @ w_in
    mqk, mv, mo, mi, mf, aq, ak, av = jnp.split(proj, IN_SPLITS_2, axis=-1)
    qk = jax.nn.silu(causal_conv(mqk, conv_w, conv_b))
    mq, mk = jnp.split(qk, 2, axis=-1)
    shp = (Bn, S, M_HEADS, M_HEAD_DIM)
    hm = mlstm_chunkwise(mq.reshape(shp), mk.reshape(shp), mv.reshape(shp), mi + b_igate, mf + b_fgate)
    hm = jax.nn.sigmoid(mo).reshape(shp) * hm.astype(h.dtype)
    hm = rms_norm_2(hm, m_norm_w).reshape(Bn, S, M_WIDTH)
    ha = diff_attention(aq.reshape(Bn, S, A_HEADS_2, 2, A_QK_DIM), ak.reshape(Bn, S, A_HEADS_2, 2, A_QK_DIM),
                        av.reshape(Bn, S, A_HEADS_2, A_HEAD_DIM), q_norm_w, k_norm_w,
                        lq1, lk1, lq2, lk2, a_norm_w, lambda_init)
    return jnp.concatenate([hm, ha], axis=-1) @ w_out

def hierarchical_moe(h, w_group, b_group, w_expert, b_expert, w_gate, w_up, w_down):
    Bn, S, D = h.shape
    T = Bn * S
    xt = h.reshape(T, D)
    f32 = jnp.float32
    g_logits = (xt @ w_group).astype(f32) + b_group.astype(f32)
    g_prob = jax.nn.softmax(g_logits, axis=-1)
    g_sel = jnp.argmax(g_logits, axis=-1)
    g_w = jnp.take_along_axis(g_prob, g_sel[:, None], axis=1)[:, 0]
    e_logits = ((xt @ w_expert).astype(f32) + b_expert.astype(f32)).reshape(T, N_GROUPS, EXPERTS_PER_GROUP)
    e_in = jnp.take_along_axis(e_logits, g_sel[:, None, None], axis=1)[:, 0]
    top_vals, top_idx = lax.top_k(e_in, TOP_K)
    weights = g_w[:, None] * jax.nn.softmax(top_vals, axis=-1)
    eid = (g_sel[:, None] * EXPERTS_PER_GROUP + top_idx).reshape(-1)
    A = T * TOP_K
    tok = jnp.arange(A) // TOP_K
    counts = jax.ops.segment_sum(jnp.ones_like(eid), eid, num_segments=N_EXPERTS)
    padded = ((counts + MOE_BLOCK - 1) // MOE_BLOCK) * MOE_BLOCK
    pad_end = jnp.cumsum(padded)
    pad_start = pad_end - padded
    start = jnp.cumsum(counts) - counts
    order = jnp.argsort(eid)
    eid_sorted = eid[order]
    dest_sorted = pad_start[eid_sorted] + (jnp.arange(A) - start[eid_sorted])
    dest = jnp.zeros((A,), jnp.int32).at[order].set(dest_sorted.astype(jnp.int32))
    P = ((A + MOE_BLOCK - 1) // MOE_BLOCK) * MOE_BLOCK + N_EXPERTS * MOE_BLOCK
    NB = P // MOE_BLOCK
    block_start = jnp.arange(NB) * MOE_BLOCK
    block_expert = jnp.minimum(jnp.sum(pad_end[None, :] <= block_start[:, None], axis=1), N_EXPERTS - 1)
    x_buf = jnp.zeros((P, D), h.dtype).at[dest].set(xt[tok])

    def expert_block(args):
        xb, e = args
        hid = jax.nn.silu(xb @ w_gate[e]) * (xb @ w_up[e])
        return hid @ w_down[e]

    y_buf = lax.map(expert_block, (x_buf.reshape(NB, MOE_BLOCK, D), block_expert)).reshape(P, D)
    y = jnp.sum(y_buf[dest].reshape(T, TOP_K, D) * weights[..., None].astype(h.dtype), axis=1)
    return y.reshape(Bn, S, D)

def second_inputs(seed: int = 0) -> dict:
    key = jax.random.key(seed)
    ks = jax.random.split(key, 24)
    nrm = jax.random.normal
    f32 = jnp.float32
    L = DEPTH
    gain = lambda k, n: 1.0 + 0.01 * nrm(k, (L, n), f32)
    return {
        'x': nrm(ks[0], (BATCH, SEQ, D_MODEL), f32),
        'norm1_w': gain(ks[1], D_MODEL),
        'w_in': nrm(ks[2], (L, D_MODEL, IN_COLS_2), f32) * D_MODEL ** -0.5,
        'b_igate': 0.1 * nrm(ks[3], (L, M_HEADS), f32),
        'b_fgate': jnp.linspace(3.0, 6.0, M_HEADS, dtype=f32)[None, :] + 0.1 * nrm(ks[4], (L, M_HEADS), f32),
        'conv_w': nrm(ks[5], (L, CONV_WIDTH, 2 * M_WIDTH), f32) * CONV_WIDTH ** -0.5,
        'conv_b': 0.01 * nrm(ks[6], (L, 2 * M_WIDTH), f32),
        'm_norm_w': gain(ks[7], M_HEAD_DIM),
        'q_norm_w': gain(ks[8], A_QK_DIM),
        'k_norm_w': gain(ks[9], A_QK_DIM),
        'lambda_q1': 0.1 * nrm(ks[10], (L, A_QK_DIM), f32),
        'lambda_k1': 0.1 * nrm(ks[11], (L, A_QK_DIM), f32),
        'lambda_q2': 0.1 * nrm(ks[12], (L, A_QK_DIM), f32),
        'lambda_k2': 0.1 * nrm(ks[13], (L, A_QK_DIM), f32),
        'a_norm_w': gain(ks[14], A_HEAD_DIM),
        'w_out': nrm(ks[15], (L, D_MIX, D_MODEL), f32) * D_MIX ** -0.5,
        'norm2_w': gain(ks[16], D_MODEL),
        'w_group': nrm(ks[17], (L, D_MODEL, N_GROUPS), f32) * D_MODEL ** -0.5,
        'b_group': 0.01 * nrm(ks[18], (L, N_GROUPS), f32),
        'w_expert': nrm(ks[19], (L, D_MODEL, N_EXPERTS), f32) * D_MODEL ** -0.5,
        'b_expert': 0.01 * nrm(ks[20], (L, N_EXPERTS), f32),
        'w_gate': nrm(ks[21], (L, N_EXPERTS, D_MODEL, D_EXPERT), f32) * D_MODEL ** -0.5,
        'w_up': nrm(ks[22], (L, N_EXPERTS, D_MODEL, D_EXPERT), f32) * D_MODEL ** -0.5,
        'w_down': nrm(ks[23], (L, N_EXPERTS, D_EXPERT, D_MODEL), f32) * D_EXPERT ** -0.5,
    }

def second_block(x, norm1_w, w_in, b_igate, b_fgate, conv_w, conv_b, m_norm_w, q_norm_w, k_norm_w,
              lambda_q1, lambda_k1, lambda_q2, lambda_k2, a_norm_w, w_out, norm2_w,
              w_group, b_group, w_expert, b_expert, w_gate, w_up, w_down):
    for l in range(DEPTH):
        lambda_init = 0.8 - 0.6 * math.exp(-0.3 * l)
        h = rms_norm_2(x, norm1_w[l])
        x = x + hybrid_mixer(h, w_in[l], b_igate[l], b_fgate[l], conv_w[l], conv_b[l], m_norm_w[l],
                             q_norm_w[l], k_norm_w[l], lambda_q1[l], lambda_k1[l], lambda_q2[l],
                             lambda_k2[l], a_norm_w[l], w_out[l], lambda_init)
        h = rms_norm_2(x, norm2_w[l])
        x = x + hierarchical_moe(h, w_group[l], b_group[l], w_expert[l], b_expert[l],
                                 w_gate[l], w_up[l], w_down[l])
    return x


def setup_inputs(seed=0):
    out = dict(first_inputs(seed))
    for name, value in second_inputs(seed + 1).items():
        if name != "x":
            out[name + "_2"] = value
    return out


def reference(
    x, positions, g_ffn1, w1_gate, w1_up, w1_down, g_mix, w_in, g_cq, w_uq_a, w_q_idx, g_q_a,
    g_k_a, w_uv_a, w_o_a, w_o_b, w_out, g_ffn2, w2_gate, w2_up, w2_down, norm1_w_2, w_in_2,
    b_igate_2, b_fgate_2, conv_w_2, conv_b_2, m_norm_w_2, q_norm_w_2, k_norm_w_2, lambda_q1_2,
    lambda_k1_2, lambda_q2_2, lambda_k2_2, a_norm_w_2, w_out_2, norm2_w_2, w_group_2, b_group_2,
    w_expert_2, b_expert_2, w_gate_2, w_up_2, w_down_2,
):
    x = first_block(
        x, positions, g_ffn1, w1_gate, w1_up, w1_down, g_mix, w_in, g_cq, w_uq_a, w_q_idx,
        g_q_a, g_k_a, w_uv_a, w_o_a, w_o_b, w_out, g_ffn2, w2_gate, w2_up, w2_down,
    )
    return second_block(
        x, norm1_w_2, w_in_2, b_igate_2, b_fgate_2, conv_w_2, conv_b_2, m_norm_w_2, q_norm_w_2,
        k_norm_w_2, lambda_q1_2, lambda_k1_2, lambda_q2_2, lambda_k2_2, a_norm_w_2, w_out_2,
        norm2_w_2, w_group_2, b_group_2, w_expert_2, b_expert_2, w_gate_2, w_up_2, w_down_2,
    )


_drawn_inputs = setup_inputs


def setup_inputs(seed=0):
    import zlib

    import numpy as np

    out = dict(_drawn_inputs(seed))
    spreads = {}
    factors = {'g_cq': 3.033,
     'g_q_a': 5.344,
     'g_k_a': 6.546,
     'g_ffn2': 3.176,
     'norm1_w_2': 2.833,
     'b_igate_2': 64.0,
     'conv_b_2': 37.592,
     'm_norm_w_2': 40.44,
     'q_norm_w_2': 5.538,
     'k_norm_w_2': 5.764,
     'lambda_k1_2': 64.0,
     'a_norm_w_2': 33.112,
     'b_group_2': 29.056,
     'b_expert_2': 39.336,
     'norm2_w_2': 8.0}
    for name, (base, spread) in spreads.items():
        noise = np.random.default_rng([zlib.crc32(name.encode()), seed]).standard_normal(out[name].shape)
        drawn = base * np.exp(spread * noise) if base else spread * noise
        out[name] = __import__('jax').numpy.asarray(drawn.astype(out[name].dtype))
    for name, factor in factors.items():
        out[name] = (out[name] * factor).astype(out[name].dtype)
    return out
```

```python
import numpy as np
import concourse.bass as bass
from concourse import mybir

F32 = mybir.dt.float32
F32R = mybir.dt.float32r
I32 = mybir.dt.int32
ALU = mybir.AluOpType
ACT = mybir.ActivationFunctionType
AX = mybir.AxisListType

NEG = -1.0e30
REPL = -3.0e38
EPS = 1e-6
CAP = 1408
NSTAGE, NSPLIT, AHEAD = 4, 3, 2
NB = 32
NX = 7
NSLOT = (NB + NX) * 128

COLS = {}


def _cols():
    at = 0
    for name, n in [("g_ffn1", 8), ("g_mix", 8), ("g_cq", 2), ("g_q_a", 1), ("g_k_a", 1), ("g_ffn2", 8),
                    ("norm1", 8), ("conv_w", 32), ("conv_b", 8), ("m_norm", 1), ("q_norm", 1), ("k_norm", 1),
                    ("a_norm", 1), ("bi", 1), ("bf", 1), ("lq1", 1), ("lq2", 1), ("lk1", 1), ("lk2", 1),
                    ("inv_freq", 1), ("sgn", 1), ("eps", 1), ("one", 1)]:
        COLS[name] = (at, n)
        at += n
    return at


NCOLS = _cols()
MATS = ["ident", "ones", "mean1024", "mean256", "mean128", "blk64", "perm", "tru", "sel0", "sel1", "sel2", "sel3", "extra"]
RMATS = ["ntri", "nones", "mstrict", "mpos", "dmask"]


def shape_constants():
    i = np.arange(128)
    r, c = i[:, None], i[None, :]
    m = {}
    m["ident"] = r == c
    m["ones"] = np.ones((128, 128))
    for d in (1024, 256, 128):
        m[f"mean{d}"] = np.full((128, 128), 1.0 / d)
    m["blk64"] = ((r // 64) == (c // 64)) / 64.0
    m["perm"] = r == np.where(c % 64 < 32, c + 32, c - 32)
    m["ntri"] = -(r >= c).astype(np.float32)
    m["nones"] = -np.ones((128, 128))
    m["mstrict"] = np.where(c > r, 0.0, NEG)
    m["mpos"] = np.where(c < r, -NEG, 0.0)
    m["tru"] = r < c
    for h in range(4):
        m[f"sel{h}"] = (r == h) & (c >= 0)
    m["dmask"] = np.where(c // 64 <= r // 64, 0.0, NEG)
    x = np.zeros((128, 128), np.float32)
    x[:, 0:32] = np.arange(32) * 128.0
    x[:, 32:36] = 4.0 - np.arange(4)
    x[:, 36:68] = 32.0 - np.arange(32)
    x[:, 68:72] = i[:, None] + 128.0 * np.arange(4)
    m["extra"] = x
    return np.stack([np.asarray(m[k], np.float32) for k in MATS + RMATS], axis=1).reshape(128, -1)


class Tok:

    def __init__(self, eng, sem=None, val=None):
        self.eng, self.sem, self.val, self.used = eng, sem, val, sem is not None


class Program:

    def __init__(self, nc, ctx):
        self.nc, self.ctx = nc, ctx
        self.q = {e: [] for e in ("pe", "act", "dve", "pool", "sp")}
        self.sem = {e: ctx.enter_context(nc.semaphore("s_" + e)) for e in self.q}
        self.counts = {}
        self.last = {}
        self.main = None
        self.regs = {}
        self.ei = None
        self.tables = None

    def op(self, eng, fn, *waits):
        t = Tok(eng)
        flat = []
        for w in waits:
            flat += [x for x in (w if isinstance(w, (list, tuple)) else [w]) if x is not None]
        for w in flat:
            w.used = True
        self.q[eng].append([fn, flat, t])
        self.last[eng] = t
        return t

    def dma(self, eng, fn, sem, *waits, n=1):
        self.counts[sem] = self.counts.get(sem, 0) + 16 * n
        flat = []
        for w in waits:
            flat += [x for x in (w if isinstance(w, (list, tuple)) else [w]) if x is not None]
        for w in flat:
            w.used = True
        self.q[eng].append([fn, flat, None])
        return Tok("dma", sem, self.counts[sem])

    def hold(self, eng):
        item = [None, [], None]
        self.q[eng].append(item)
        return item

    def barrier(self, engs=("pe", "act", "dve", "pool"), also=()):
        toks = [self.last[e] for e in engs if e in self.last]
        for e in engs:
            ts = [t for t in toks if t.eng != e or e != "pe"] + list(also)
            for t in ts:
                t.used = True
            self.q[e].append([None, ts, None])

    def region_begin(self):
        self.main = (self.q, self.last)
        self.q, self.last = {e: [] for e in self.q}, {}
        self.tables = None

    def region_end(self, n):
        inner = self.q
        self.q, self.last = self.main
        self.main = self.tables = None
        for e in self.q:
            self.q[e].append(("region", inner[e], n))

    def emit(self, block):
        inner = {e: self.ctx.enter_context(self.nc.semaphore("x_" + e)) for e in self.q}
        for e, items in self.q.items():
            n = m = 0
            for it in items:
                if it[0] == "region":
                    for fn, waits, tok in it[1]:
                        if tok is not None and tok.used:
                            m += 1
                            tok.sem, tok.val = inner[e], m
                elif it[2] is not None and it[2].used:
                    n += 1
                    it[2].sem, it[2].val = self.sem[e], n
        for e, deco in (("pe", block.tensor), ("act", block.scalar), ("dve", block.vector),
                        ("pool", block.gpsimd), ("sp", block.sync)):
            def body(eng, e=e):
                seen = {}

                def run(items):
                    for fn, waits, tok in items:
                        for w in waits:
                            if w.eng == e and e == "pe":
                                continue
                            if seen.get(id(w.sem), 0) < w.val:
                                seen[id(w.sem)] = w.val
                                eng.wait_ge(w.sem, w.val)
                        if fn is not None:
                            ins = fn(eng)
                            if tok is not None and tok.used:
                                ins.then_inc(tok.sem, 1)
                regs = None
                for it in self.q[e]:
                    if it[0] != "region":
                        run([it])
                        continue
                    if regs is None:
                        regs = [eng.value_load(self.ei[0:1, 7:8], min_val=0, max_val=NX)]
                        if e == "sp":
                            self.regs = {x: eng.value_load(self.ei[0:1, x:x + 1], min_val=0, max_val=NB - 1) for x in range(NX)}
                    kept = dict(seen)
                    with eng.If(regs[0] > it[2]):
                        run(it[1])
                    seen.clear()
                    seen.update(kept)
            deco(body)


class Bank:
    def __init__(self, t):
        self.t, self.free = t, []


def build(nc, A, out):
    from contextlib import ExitStack
    ctx = ExitStack()
    with ctx:
        P = Program(nc, ctx)
        op, dma = P.op, P.dma
        place = [(nc.sbuf_base + 63) // 64 * 64]
        names = [0]

        def sb(shape, dt=F32, name="t"):
            names[0] += 1
            size = int(np.prod(shape[1:])) * 4
            t = nc.alloc_sbuf_tensor_at(f"{name}_{names[0]}", shape, dt, offset=place[0])
            place[0] += (size + 63) // 64 * 64
            assert place[0] <= nc.sbuf_usable_end, (name, place[0], nc.sbuf_usable_end)
            return t

        def pair(shape, name="t"):
            return sb(shape, F32R, name + "H"), sb(shape, F32R, name + "L")

        def sem(name):
            names[0] += 1
            return ctx.enter_context(nc.semaphore(f"{name}{names[0]}"))

        banks = [Bank(ctx.enter_context(nc.psum_tensor(f"bank{i}", [128, 512], F32))) for i in range(8)]
        turn = [0]

        def bank():
            turn[0] = (turn[0] + 1) % 8
            return banks[turn[0]]

        sets = {"log_exp": "natural_log_exp_and_others", "silu": "silu_and_others", "sigmoid": "sigmoid_and_others",
                "trig": "trig_and_small"}

        def tables(name):
            if P.tables != name:
                P.tables = name
                op("act", lambda e: e.preload_act_table_set(sets[name]))

        x_place = place[0]
        xT = sb([128, 8, 512], F32, "xT")
        hH, hL = pair([128, 8, 512], "h")
        stage = [sb([128, CAP], F32, f"stage{i}") for i in range(NSTAGE)]
        wH = [sb([128, CAP], F32R, f"wH{i}") for i in range(NSPLIT)]
        wL = [sb([128, CAP], F32R, f"wL{i}") for i in range(NSPLIT)]
        cols = sb([128, NCOLS], F32, "cols")
        mats = sb([128, len(MATS), 128], F32, "mats")
        rmats = sb([128, len(RMATS), 128], F32R, "rmats")
        rident, rones = sb([128, 128], F32R, "rident"), sb([128, 128], F32R, "rones")
        rpos, rdm = rmats[:, 3, :], rmats[:, 4, :]
        mark0 = place[0]

        def col(name, k=0):
            at = COLS[name][0] + k
            return cols[:, at:at + 1]

        def mat(name):
            return mats[:, MATS.index(name), :]

        s_c = sem("s_c")
        dma("sp", lambda e: e.dma_start(cols[:, :], A["cols"]).then_inc(s_c, 16), s_c)
        dma("sp", lambda e: e.dma_start(xT[:, :, :], A["x"]).then_inc(s_c, 16), s_c)
        nm = len(MATS) * 128
        rstage = nc.alloc_sbuf_tensor_at("rstage", [128, len(RMATS) * 128], F32, offset=nc.sbuf_usable_end // 64 * 64 - 16384)
        dma("sp", lambda e: e.dma_start(rstage[:, :], A["mats"][:, nm:]).then_inc(s_c, 16), s_c)
        t_c = dma("sp", lambda e: e.dma_start(mats[:, :, :].rearrange("p a b -> p (a b)"), A["mats"][:, 0:nm]).then_inc(s_c, 16), s_c)
        op("act", lambda e: e.activation(rmats[:, :, :].rearrange("p a b -> p (a b)"), rstage[:, :], ACT.Copy), t_c)
        op("act", lambda e: e.activation(rident[:, :], mat("ident"), ACT.Copy), t_c)
        t_r = t_rp = op("act", lambda e: e.activation(rones[:, :], mat("ones"), ACT.Copy), t_c)
        xb_d = nc.dram_tensor("slot_rows", (NSLOT, 1024), F32).ap()
        yb_d = nc.dram_tensor("slot_results", (NSLOT, 1024), F32).ap()
        top_end = nc.sbuf_usable_end // 64 * 64 - 4096
        zero = nc.alloc_sbuf_tensor_at("zero", [128, 1024], F32, offset=top_end - 4096)
        s_z = sem("s_z")
        t_zero = [op("pool", lambda e: e.memset(zero[:, :], 0.0))]
        zeros = [xb_d[n * 128:(n + 1) * 128, :] for n in range(NB + NX)] + [yb_d[n * 128:(n + 1) * 128, :] for n in range(NB, NB + NX)]

        def store_zeros(n, *waits):
            for d in [zeros.pop() for _ in range(min(n, len(zeros)))]:
                t_zero.append(dma("pool", lambda e, d=d: e.dma_start(d, zero[:, :]).then_inc(s_z, 16), s_z, t_zero[0], *waits))

        class Slot:
            def __init__(self, *t):
                self.t, self.sem, self.user, self.after = t, sem("s_stage"), None, []

        stream = {"stage": [Slot(t) for t in stage], "split": [Slot(a, b) for a, b in zip(wH, wL)], "ahead": AHEAD}
        units = []
        holes = []

        class Unit:
            pass

        def use(parts, k, n, ahead=True):
            i = len(units)
            u = Unit()
            size = k * n
            assert size <= CAP
            u.t_hi, u.t_lo, u.done = Tok("act"), Tok("dve"), None
            st_, sp_ = stream["stage"].pop(0), stream["split"].pop(0)
            stream["stage"].append(st_)
            stream["split"].append(sp_)
            s, slot = st_.sem, st_.t[0]
            dst_hi, dst_lo = sp_.t
            before = ([t for t in (st_.user.t_lo, st_.user.t_hi) if t] if st_.user else []) + st_.after
            reader = ([sp_.user.done] if sp_.user and sp_.user.done else []) + sp_.after
            st_.user = sp_.user = u
            st_.after, sp_.after = [], []

            def go(e):
                for at, src in parts:
                    src = src(e) if callable(src) else src
                    a, b = src.shape[-2], src.shape[-1]
                    e.dma_start(slot[:, at:at + a * b].rearrange("p (a b) -> p a b", a=a), src).then_inc(s, 16)
            u.landed = dma("sp", go, s, before, n=len(parts))
            while len(holes) <= (i + stream["ahead"] if ahead else i):
                holes.append((P.hold("act"), P.hold("dve")))
            for t in reader + [u.t_hi, u.t_lo]:
                t.used = True
            holes[i][0][:] = [lambda e: e.activation(dst_hi[:, 0:size], slot[:, 0:size], ACT.Copy), [u.landed] + reader, u.t_hi]
            holes[i][1][:] = [lambda e: e.tensor_tensor(dst_lo[:, 0:size], slot[:, 0:size], dst_hi[:, 0:size].bitcast(F32),
                                                        ALU.subtract), reader + [u.t_hi], u.t_lo]
            units.append(u)
            u.H = dst_hi[:, 0:size].rearrange("p (k n) -> p k n", k=k)
            u.L = dst_lo[:, 0:size].rearrange("p (k n) -> p k n", k=k)
            return u

        def mm(outp, lhsT, rhs, start, stop, *waits, skip=False):
            return op("pe", lambda e: e.matmul(outp, lhsT, rhs, start=start, stop=stop, skip_group_check=skip), *waits)

        def mm3(outp, a, b, start, stop, *waits, skip=False):
            mm(outp, a[0], b[0], start, False, *waits, skip=skip)
            mm(outp, a[0], b[1], False, False, skip=skip)
            return mm(outp, a[1], b[0], False, stop, skip=skip)

        def split(src, H, L, *waits, scale=1.0):
            t1 = op("act", lambda e: e.activation(H, src, ACT.Copy, scale=scale), *waits)
            if scale == 1.0:
                return op("dve", lambda e: e.tensor_tensor(L, src, H.bitcast(F32), ALU.subtract), t1, *waits)
            return op("dve", lambda e: e.scalar_tensor_tensor(L, src, scale, H.bitcast(F32), ALU.mult, ALU.subtract), t1, *waits)

        def dense(parts, K, act, *waits, b=None, parts_ready=None):
            u = use(parts, K, 128)
            b = b or bank()
            w = [u.t_lo, u.t_hi, b.free, list(waits)]
            for k in range(K):
                last = mm3(b.t[:, :], (u.H[:, k, :], u.L[:, k, :]), (act[0][:, k, :], act[1][:, k, :]),
                           k == 0, k == K - 1, *(w if k == 0 else ()), *([parts_ready[k]] if parts_ready else ()))
            u.done = last
            return b, last

        def wcols(name, c0, n, k0=0, K=8):
            v = A[name].rearrange("(k p) n -> p k n", p=128)
            return v[:, k0:k0 + K, c0:c0 + n]

        tmp = {}

        class Ring:
            def __init__(self, n, shape, dt=F32, name="r"):
                self.t = [sb(shape, dt, name) for _ in range(n)]
                self.free = [[] for _ in range(n)]
                self.i = -1

            def get(self):
                self.i = (self.i + 1) % len(self.t)
                f = self.free[self.i]
                self.free[self.i] = []
                return self.t[self.i], f, self

            def release(self, *toks):
                self.free[self.i] = list(toks)

        def rings(ny=3):
            tmp["sq"] = Ring(2, [128, 512], name="sq")
            tmp["rr"] = Ring(2, [128, 512], name="rr")
            tmp["y"] = Ring(ny, [128, 512], name="y")

        acc = nc.alloc_sbuf_tensor_at("acc", [128, 512], F32, offset=top_end)
        xsq = nc.alloc_sbuf_tensor_at("xsq", [128, 512], F32, offset=top_end + 2048)
        summed = {"t": None, "n": 0}

        def add_square(k, *waits):
            first = summed["n"] % 8 == 0
            dst = acc if first else xsq
            t = op("act", lambda e: e.activation(dst[:, :], xT[:, k, :], ACT.Square), summed["t"], *waits)
            if not first:
                t = op("dve", lambda e: e.tensor_tensor(acc[:, :], acc[:, :], xsq[:, :], ALU.add), t)
            summed["t"], summed["n"] = t, summed["n"] + 1

        def norm_x(gain):
            b = bank()
            t = mm(b.t[:, :], mat("mean1024"), acc[:, :], True, True, summed["t"], b.free, t_c)
            r, f, _ = tmp["rr"].get()
            tables("log_exp")
            t1 = op("act", lambda e: e.activation(r[:, :], b.t[:, :], ACT.Ln, bias=col("eps")), t, f, t_c)
            b.free = [t1]
            summed["t"] = t1
            tables("log_exp")
            t2 = op("act", lambda e: e.activation(r[:, :], r[:, :], ACT.Exp, scale=-0.5), t1)
            ts = []
            for k in range(8):
                y, f, _ = tmp["y"].get()
                t3 = op("dve", lambda e, y=y, k=k: e.scalar_tensor_tensor(y[:, :], xT[:, k, :], col(gain, k), r[:, :], ALU.mult, ALU.mult), t2, f)
                ts.append(split(y[:, :], hH[:, k, :], hL[:, k, :], t3, P.last.get("pe") if k == 0 else None))
                tmp["y"].release(ts[-1])
            tmp["rr"].release(t3)
            return ts

        def rms(src, K, ones, *waits):
            sq, rr = tmp["sq"], tmp["rr"]
            b = bank()
            for k in range(K):
                s, f, _ = sq.get()
                t1 = op("act", lambda e, s=s, k=k: e.activation(s[:, :], src(k), ACT.Square), f, *waits)
                last = mm(b.t[:, :], ones, s[:, :], k == 0, k == K - 1, t1, b.free, t_c)
                sq.release(last)
            r, f, _ = rr.get()
            tables("log_exp")
            t1 = op("act", lambda e: e.activation(r[:, :], b.t[:, :], ACT.Ln, bias=col("eps")), last, f, t_c)
            b.free = [t1]
            tables("log_exp")
            return r, op("act", lambda e: e.activation(r[:, :], r[:, :], ACT.Exp, scale=-0.5), t1)

        def norm(src, K, ones, gain, out, *waits):
            r, t2 = rms(src, K, ones, *waits)
            for k in range(K):
                y, f, _ = tmp["y"].get()
                t3 = op("dve", lambda e, y=y, k=k: e.scalar_tensor_tensor(y[:, :], src(k), gain(k), r[:, :], ALU.mult, ALU.mult), t2, f, t_c, *waits)
                t4 = split(y[:, :], out[0][:, k, :], out[1][:, k, :], t3)
                tmp["y"].release(t4)
            tmp["rr"].release(t3)
            return t4

        def chunk_norm(b, t, ones, gain, out, scale=1.0, rope=None, before=()):
            y, f, _ = tmp["y"].get()
            ty = op("act", lambda e: e.activation(y[:, :], b.t[:, :], ACT.Copy), t, f)
            b.free = [ty]
            if gain is not None:
                r, t2 = rms(lambda k: y[:, :], 1, ones, ty)
                ty = op("dve", lambda e: e.scalar_tensor_tensor(y[:, :], y[:, :], gain, r[:, :], ALU.mult, ALU.mult), t2, t_c)
                tmp["rr"].release(ty)
            if rope is not None:
                cs, sn, tr = rope
                b2 = bank()
                t2 = mm(b2.t[:, :], mat("perm"), y[:, :], True, True, ty, b2.free, t_c)
                z, f, _ = tmp["sq"].get()
                t3 = op("dve", lambda e: e.tensor_tensor(z[:, :], b2.t[:, :], sn[:, :], ALU.mult), t2, f, tr)
                b2.free = [t3]
                t4 = op("dve", lambda e: e.tensor_tensor(y[:, :], y[:, :], cs[:, :], ALU.mult), t2, ty, tr)
                ty = op("dve", lambda e: e.tensor_tensor(y[:, :], y[:, :], z[:, :], ALU.add), t3, t4)
                tmp["sq"].release(ty)
            t5 = split(y[:, :], out[0], out[1], ty, list(before), scale=scale)
            tmp["y"].release(t5)
            return t5

        def ffn(gate, up, down, gain):
            place[0] = mark0
            rings()
            hid = pair([128, 11, 512], "hid")
            sg = Ring(2, [128, 512], name="sg")
            hf = Ring(3, [128, 512], name="hf")
            ths = norm_x(gain)
            t_down = None
            for half in range(2):
                for m in range(11):
                    c0 = (half * 11 + m) * 128
                    bg, tg = dense([(0, wcols(gate, c0, 128))], 8, h, parts_ready=ths if m == 0 and half == 0 else None)
                    bu, tu = dense([(0, wcols(up, c0, 128))], 8, h)
                    s, f, _ = sg.get()
                    tables("silu")
                    t1 = op("act", lambda e, s=s, b=bg: e.activation(s[:, :], b.t[:, :], ACT.Silu), tg, f)
                    bg.free = [t1]
                    y, f, _ = hf.get()
                    t2 = op("dve", lambda e, y=y, s=s, b=bu: e.tensor_tensor(y[:, :], s[:, :], b.t[:, :], ALU.mult), t1, tu, f)
                    bu.free = [t2]
                    sg.release(t2)
                    t3 = split(y[:, :], hid[0][:, m, :], hid[1][:, m, :], t2, t_down)
                    hf.release(t3)
                    store_zeros(3, t3)
                for m in range(8):
                    b, t_down = dense([(0, wcols(down, m * 128, 128, half * 11, 11))], 11, hid, t3)
                    tx = op("dve", lambda e, b=b, m=m: e.scalar_tensor_tensor(xT[:, m, :], b.t[:, :], 0.5, xT[:, m, :], ALU.mult, ALU.add), t_down)
                    b.free = [tx]
                    if half == 1:
                        add_square(m, tx)
            P.barrier(also=t_zero[-1:])
            return tx

        REG = [(0, 0, 0), (1, 0, 512), (2, 0, 1024), (1, 384, 896)]

        def token_rows(unit_parts, n, dst_banks, act, *waits):
            for kk in range(4):
                u = use([(0, unit_parts(kk))], 2, n)
                for tt in range(4):
                    for j in range(2):
                        k = 2 * kk + j
                        last = mm3(dst_banks[tt].t[:, 0:n], (act[0][:, k, tt * 128:(tt + 1) * 128], act[1][:, k, tt * 128:(tt + 1) * 128]),
                                   (u.H[:, j, :], u.L[:, j, :]), k == 0, k == 7,
                                   *([u.t_lo, u.t_hi, dst_banks[tt].free, list(waits)] if j == 0 else []))
                u.done = last
            return last

        def load(dst, src, *waits):
            s = sem("s_ld")
            return dma("pool", lambda e: e.dma_start(dst, src).then_inc(s, 16), s, *waits)

        def mixer1():
            place[0] = mark0
            cq = pair([128, 2, 512], "cq")
            cqf = sb([128, 2, 512], F32, "cqf")
            cs, sn = sb([128, 512], F32, "cs"), sb([128, 512], F32, "sn")
            place[0] = mark0
            ya = pair([128, 4, 512], "ya")
            mark1 = place[0]
            qa = pair([128, 4, 512], "qa")
            ka = pair([128, 512], "ka")
            va = pair([128, 4, 128], "va")
            amask = sb([128, 1280], F32R, "amask")
            widx = sb([128, 4, 8], F32, "widx")
            wuv = pair([128, 4, 128], "wuv")
            mark2 = place[0]
            rings()
            qi = pair([128, 4, 512], "qi")
            ki = pair([128, 512], "ki")
            at = place[0]
            wuvF = sb([128, 8, 64], F32, "wuvF")
            posi = sb([128, 512], I32, "posi")
            ang = sb([128, 512], F32, "ang")
            nn = sb([128, 512], F32, "nn")
            place[0] = at

            ths = norm_x("g_mix")
            tw = load(wuvF[:, :, :], A["w_uv_a"].rearrange("h c d -> c h d"), P.last["act"], P.last["dve"], P.last["pe"])
            split(wuvF[:, :, :].rearrange("p (a b) d -> p a (b d)", b=2), wuv[0][:, :, :], wuv[1][:, :, :], tw)
            tp = load(posi[:, :], A["positions"].partition_broadcast(128).rearrange("p a n -> p (a n)"))
            t = op("dve", lambda e: e.tensor_copy(ang[:, :], posi[:, :]), tp)
            t = op("dve", lambda e: e.tensor_scalar(ang[:, :], ang[:, :], col("inv_freq"), None, ALU.mult), t, t_c)
            magic = 12582912.0
            t = op("dve", lambda e: e.tensor_scalar(nn[:, :], ang[:, :], float(1 / (2 * np.pi)), magic, ALU.mult, ALU.add), t)
            t = op("dve", lambda e: e.tensor_scalar(nn[:, :], nn[:, :], magic, None, ALU.subtract), t)
            c1 = 6.28125
            c2 = float(np.float32(np.round((2 * np.pi - c1) * 2 ** 21) / 2 ** 21))
            c3 = float(2 * np.pi - c1 - c2)
            for c in (c1, c2, c3):
                t = op("dve", lambda e, c=c: e.scalar_tensor_tensor(ang[:, :], nn[:, :], -c, ang[:, :], ALU.mult, ALU.add), t)
            t = op("dve", lambda e: e.tensor_scalar(ang[:, :], ang[:, :], 3.1415925, -3.1415925, ALU.min, ALU.max), t)
            tables("trig")
            t1 = op("act", lambda e: e.activation(sn[:, :], ang[:, :], ACT.Sin), t)
            tables("trig")
            t2 = op("act", lambda e: e.activation(cs[:, :], ang[:, :], ACT.Sin, scale=0.5), t)
            t = op("dve", lambda e: e.tensor_tensor(cs[:, :], cs[:, :], cs[:, :], ALU.mult), t2)
            t = op("dve", lambda e: e.tensor_scalar(cs[:, :], cs[:, :], -2.0, 1.0, ALU.mult, ALU.add), t)
            t = op("dve", lambda e: e.tensor_scalar(sn[:, :], sn[:, :], col("sgn"), None, ALU.mult), t1, t)
            rope = (cs, sn, t)

            for m in range(2):
                b, t = dense([(0, wcols("w_in", m * 128, 128))], 8, h, parts_ready=ths if m == 0 else None)
                tq = op("act", lambda e, b=b, m=m: e.activation(cqf[:, m, :], b.t[:, :], ACT.Copy), t)
                b.free = [tq]
            bk, tk = dense([(0, wcols("w_k2", 128, 128))], 8, h)
            tki = chunk_norm(bk, tk, None, None, (ki[0][:, :], ki[1][:, :]), rope=rope)
            tcq = norm(lambda k: cqf[:, k, :], 2, mat("mean256"), lambda k: col("g_cq", k), cq, tq)
            vb4 = [banks[i] for i in range(4)]
            tv = token_rows(lambda kk: wcols("w_vw", 0, 136, 2 * kk, 2), 136, vb4, h)
            for tt in range(4):
                t1 = split(vb4[tt].t[:, 0:128], va[0][:, tt, :], va[1][:, tt, :], tv)
                t2 = op("dve", lambda e, tt=tt: e.tensor_scalar(widx[:, tt, :], vb4[tt].t[:, 128:136], float((8 ** -0.5) * (64 ** -0.5)), None, ALU.mult), t1)
                vb4[tt].free = [t2]
            tva = t2
            bt, tt_ = dense([(0, wcols("w_k2", 0, 128))], 8, h)
            tka = chunk_norm(bt, tt_, mat("blk64"), col("g_k_a"), (ka[0][:, :], ka[1][:, :]), rope=rope)
            for m in range(4):
                b, t = dense([(0, wcols("w_q_idx", m * 128, 128, 0, 2))], 2, cq, tcq)
                tqi = chunk_norm(b, t, None, None, (qi[0][:, m, :], qi[1][:, m, :]), rope=rope)
            for m in range(4):
                b, t = dense([(0, wcols("w_uq_a", m * 128, 128, 0, 2))], 2, cq)
                tqa = chunk_norm(b, t, mat("blk64"), col("g_q_a"), (qa[0][:, m, :], qa[1][:, m, :]), scale=0.125, rope=rope)
            W0 = [0, 128, 384, 768]
            sc = [None] + [sb([128, 128 * (i + 1)], F32, "score") for i in range(1, 4)]
            rl = Ring(2, [128, 512], name="rl")
            top = sb([128, 8], F32, "top")
            t = op("act", lambda e: e.activation(amask[:, 0:128], mat("tru"), ACT.Copy, scale=NEG), t_c, P.last["dve"])
            tm = [t, None, None, None]
            for i in range(1, 4):
                W = 128 * (i + 1)
                for hd in range(8):
                    c, po = hd // 2, 64 * (hd % 2)
                    b = bank()
                    t1 = mm3(b.t[:, 0:W], [x[po:po + 64, c, i * 128:(i + 1) * 128] for x in qi],
                             [x[po:po + 64, 0:W] for x in ki], True, True, tqi, tki, b.free)
                    r, f, _ = rl.get()
                    t2 = op("act", lambda e, r=r, b=b, W=W: e.activation(r[:, 0:W], b.t[:, 0:W], ACT.Relu), t1, f)
                    b.free = [t2]
                    if hd == 0:
                        t3 = op("dve", lambda e, r=r, i=i, W=W, hd=hd: e.tensor_scalar(sc[i][:, :], r[:, 0:W], widx[:, i, hd:hd + 1], None, ALU.mult), t2, tva)
                    else:
                        t3 = op("dve", lambda e, r=r, i=i, W=W, hd=hd: e.scalar_tensor_tensor(sc[i][:, :], r[:, 0:W], widx[:, i, hd:hd + 1], sc[i][:, :], ALU.mult, ALU.add), t2, t3)
                    rl.release(t3)
                t3 = op("dve", lambda e, i=i: e.scalar_tensor_tensor(sc[i][:, i * 128:], mat("tru"), NEG, sc[i][:, i * 128:], ALU.mult, ALU.add), t3)
                tm[i] = t3
            for i in range(1, 4):
                t = tm[i]
                for rnd in range(16):
                    t = op("dve", lambda e, i=i: e.max(top[:, :], sc[i][:, :]), t)
                    t = op("dve", lambda e, i=i: e.match_replace(sc[i][:, :], top[:, :], sc[i][:, :], REPL), t)
                W = 128 * (i + 1)
                tm[i] = op("dve", lambda e, i=i, W=W: e.tensor_scalar(amask[:, W0[i]:W0[i] + W], sc[i][:, :], -2.0e38, NEG, ALU.is_gt, ALU.mult), t)
            P.barrier()

            place[0] = mark2
            PT = [pair([128, 4, 4, 128], "PT") for _ in range(2)]
            ptfree = [[], []]
            pr = Ring(3, [128, 512], name="p")
            ol = [pair([128, 512], "ol")] * 2
            olfree = [[], []]
            st = sb([128, 64, 2], F32, "st")
            jobs = [(i, g, hh) for i in range(4) for g in range(2) for hh in range(4)]
            ready = {}

            def softmax_rows(b, t, W, p, f, n):
                t1 = op("dve", lambda e: e.tensor_reduce(st[:, n, 0:1], b.t[:, 0:W], AX.X, ALU.max), t)
                t1 = op("dve", lambda e: e.tensor_scalar(st[:, n, 0:1], st[:, n, 0:1], -1.0, None, ALU.mult), t1)
                tables("log_exp")
                t2 = op("act", lambda e: e.activation(p[:, 0:W], b.t[:, 0:W], ACT.Exp, bias=st[:, n, 0:1], accum_out=st[:, n, 1:2]), t1, f)
                b.free = [t2]
                return op("dve", lambda e: e.reciprocal(st[:, n, 1:2], st[:, n, 1:2]), t2)

            def first(n):
                i, g, hh = jobs[n]
                hd = 4 * g + hh
                c, po, W = hd // 2, 64 * (hd % 2), 128 * (i + 1)
                b = bank()
                mm(b.t[:, 0:W], rident[:, :], amask[:, W0[i]:W0[i] + W], True, False, b.free, tm[i], t_r)
                t = mm3(b.t[:, 0:W], [x[po:po + 64, c, i * 128:(i + 1) * 128] for x in qa],
                        [x[po:po + 64, 0:W] for x in ka], False, True)
                p, f, _ = pr.get()
                t2 = softmax_rows(b, t, W, p, f, n)
                t3 = op("dve", lambda e: e.tensor_scalar(p[:, 0:W], p[:, 0:W], st[:, n, 1:2], None, ALU.mult), t2)
                ready[n] = (p, t3)

            def second(n):
                i, g, hh = jobs[n]
                p, t = ready.pop(n)
                b = bank()
                for s in range(i + 1):
                    t1 = op("pe", lambda e, s=s, b=b: e.transpose(b.t[:, s * 128:(s + 1) * 128], p[:, s * 128:(s + 1) * 128], mat("ident")), t, b.free)
                pr.free[n % 3] = [t1]
                k = (n // 4) % 2
                src = b.t[:, 0:128 * (i + 1)].rearrange("p (s n) -> p s n", n=128)
                t2 = split(src, PT[k][0][:, 0:i + 1, hh, :], PT[k][1][:, 0:i + 1, hh, :], t1, ptfree[k])
                b.free = [t2]
                if hh < 3:
                    return
                b = bank()
                for s in range(i + 1):
                    t3 = mm3(b.t[:, :], (va[0][:, s, :], va[1][:, s, :]),
                             [x[:, s, :, :] for x in PT[k]], s == 0, s == i, t2, b.free)
                ptfree[k] = [t3]
                t4 = split(b.t[:, :], ol[k][0][:, :], ol[k][1][:, :], t3, olfree[0])
                b.free = [t4]
                for c2 in range(2):
                    c = 2 * g + c2
                    b = bank()
                    for e2 in range(2):
                        o = e2 * 128
                        t5 = mm3(b.t[:, o:o + 128], (wuv[0][:, c, :], wuv[1][:, c, :]),
                                 [x[:, (2 * c2 + e2) * 128:(2 * c2 + e2 + 1) * 128] for x in ol[k]], True, True, t4, b.free, skip=True)
                    for e2 in range(2):
                        pp = slice(64 * e2, 64 * e2 + 64)
                        t6 = split(b.t[pp, 128 * e2:128 * e2 + 128], ya[0][pp, c, i * 128:(i + 1) * 128], ya[1][pp, c, i * 128:(i + 1) * 128], t5)
                    b.free = [t6]
                    olfree[0] = [t5]
                return t6

            for n in range(len(jobs) + 2):
                if n < len(jobs):
                    first(n)
                if n >= 2:
                    tya = second(n - 2)
            P.barrier()

            place[0] = mark1
            yb = pair([128, 4, 512], "yb")
            vb = pair([128, 4, 512], "vb")
            qb = [pair([128, 512], "qb") for _ in range(2)]
            kb = [pair([128, 512], "kb") for _ in range(2)]
            T = [sb([128, 1280], F32, "T") for _ in range(2)]
            SP = [pair([128, 1280], "SP") for _ in range(2)]
            vbanks = banks[0:4]
            t = token_rows(lambda kk: wcols("w_in", 1544, 512, 2 * kk, 2), 512, vbanks, h)
            for tt in range(4):
                tvb = split(vbanks[tt].t[:, :], vb[0][:, tt, :], vb[1][:, tt, :], t)
                vbanks[tt].free = [tvb]
            zb = [banks[0:3], banks[3:6]]
            pvb = banks[6:8]
            z_t, s_t, a_t, qk_t = {}, {}, {}, {}
            qkfree = [[], []]
            spfree = [[], []]

            def project(c):
                bq, tq = dense([(0, wcols("w_in", 520 + c * 128, 128))], 8, h, b=pvb[0])
                t1 = split(bq.t[:, :], qb[c % 2][0][:, :], qb[c % 2][1][:, :], tq, qkfree[c % 2], scale=0.125)
                bq.free = [t1]
                bk2, tk2 = dense([(0, wcols("w_in", 1032 + c * 128, 128))], 8, h, b=pvb[1])
                t2 = split(bk2.t[:, :], kb[c % 2][0][:, :], kb[c % 2][1][:, :], tk2, qkfree[c % 2])
                bk2.free = [t2]
                qk_t[c] = [t1, t2]

            def b1(hd):
                c, po, z = hd // 2, slice(64 * (hd % 2), 64 * (hd % 2) + 64), zb[hd % 2]
                for j in range(4):
                    bk_, off, _ = REG[j]
                    N = 512 - 128 * j
                    o = z[bk_].t[:, off:off + N]
                    mm3(o, [x[po, 128 * j:128 * j + 128] for x in kb[c % 2]], [x[po, 128 * j:512] for x in qb[c % 2]],
                        j != 3, False, qk_t[c], z[bk_].free, skip=True)
                    t = mm(z[bk_].t[:, off:off + 128], rident[:, :], rmats[:, 2, :], False, True, t_r, skip=True)
                qkfree[c % 2] = [t]
                x = T[hd % 2]
                for bk_, o, n in ((0, 0, 512), (1, 512, 512), (2, 1024, 256)):
                    t1 = op("act", lambda e, bk_=bk_, o=o, n=n: e.activation(x[:, o:o + n], z[bk_].t[:, 0:n], ACT.Abs), t, spfree[hd % 2])
                tables("log_exp")
                t1 = op("act", lambda e: e.activation(x[:, :], x[:, :], ACT.Exp, scale=-1.0), t1)
                tables("log_exp")
                t1 = op("act", lambda e: e.activation(x[:, :], x[:, :], ACT.Ln, bias=col("one")), t1, t_c)
                for bk_, o, n in ((0, 0, 512), (1, 512, 512), (2, 1024, 256)):
                    t2 = op("dve", lambda e, bk_=bk_, o=o, n=n: e.scalar_tensor_tensor(x[:, o:o + n], z[bk_].t[:, 0:n], 0.0, x[:, o:o + n], ALU.max, ALU.add), t1)
                s_t[hd] = split(x[:, :], SP[hd % 2][0][:, :], SP[hd % 2][1][:, :], t2, spfree[hd % 2])

            def b2(hd):
                z, sp, x = zb[hd % 2], SP[hd % 2], T[hd % 2]
                for j in range(4):
                    bk_, off, o = REG[j]
                    for j2 in range(j, 4):
                        o2, N = REG[j2][2], 512 - 128 * j2
                        w = rmats[:, 0, :] if j2 == j else rmats[:, 1, :]
                        d = z[bk_].t[:, off + 128 * (j2 - j):off + 128 * (j2 - j) + N]
                        for part in sp:
                            t = mm(d, w, part[:, o2:o2 + N], False, True, s_t[hd], skip=True)
                for bk_, o, n in ((0, 0, 512), (1, 512, 512), (2, 1024, 256)):
                    tables("log_exp")
                    t1 = op("act", lambda e, bk_=bk_, o=o, n=n: e.activation(x[:, o:o + n], z[bk_].t[:, 0:n], ACT.Exp), t, s_t[hd])
                for bb in z:
                    bb.free = [t1]
                a_t[hd] = split(x[:, :], sp[0][:, :], sp[1][:, :], t1, t)

            def b3(hd):
                c, pp = hd // 2, slice(64 * (hd % 2), 64 * (hd % 2) + 64)
                b, a = pvb[hd % 2], SP[hd % 2]
                for j in range(4):
                    o, N = REG[j][2], 512 - 128 * j
                    t = mm3(b.t[:, 128 * j:512], (vb[0][:, j, c * 128:(c + 1) * 128], vb[1][:, j, c * 128:(c + 1) * 128]),
                            [v[:, o:o + N] for v in a], j == 0, j == 3, a_t[hd], tvb, b.free)
                spfree[hd % 2] = [t]
                t1 = split(b.t[pp, :], yb[0][pp, c, :], yb[1][pp, c, :], t)
                b.free = [t1]
                return t1

            project(0)
            for hd in range(10):
                if hd < 8:
                    if hd % 2 == 0 and hd < 6:
                        project(hd // 2 + 1)
                    if hd >= 2:
                        tyb = b3(hd - 2)
                    b1(hd)
                else:
                    tyb = b3(hd - 2)
                if 1 <= hd <= 8:
                    b2(hd - 1)
            P.barrier()

            place[0] = mark1 + (1 << 14)
            mg = pair([128, 8, 512], "mg")
            sg = Ring(2, [128, 512], name="sg")
            mt = Ring(2, [128, 512], name="mt")
            for m in range(8):
                bga, tga = dense([(0, wcols("w_in", 2056 + m * 128, 128))], 8, h)
                bgb, tgb = dense([(0, wcols("w_in", 3080 + m * 128, 128))], 8, h)
                u = use([(0, wcols("w_o_a", m * 128, 128, 0, 4)), (512, wcols("w_o_b", m * 128, 128, 0, 4))], 8, 128)
                ba, bb = bank(), bank()
                for k in range(4):
                    ta = mm3(ba.t[:, :], (u.H[:, k, :], u.L[:, k, :]), (ya[0][:, k, :], ya[1][:, k, :]), k == 0, k == 3, u.t_lo, u.t_hi, ba.free)
                for k in range(4):
                    tb = mm3(bb.t[:, :], (u.H[:, 4 + k, :], u.L[:, 4 + k, :]), (yb[0][:, k, :], yb[1][:, k, :]), k == 0, k == 3, bb.free)
                u.done = tb
                s1, f1, _ = sg.get()
                tables("sigmoid")
                t1 = op("act", lambda e, s=s1, b=bga: e.activation(s[:, :], b.t[:, :], ACT.Sigmoid), tga, f1)
                bga.free = [t1]
                y, f, _ = mt.get()
                t2 = op("dve", lambda e, s=s1, b=ba, y=y: e.tensor_tensor(y[:, :], s[:, :], b.t[:, :], ALU.mult), t1, ta, f)
                ba.free = [t2]
                sg.release(t2)
                s2, f2, _ = sg.get()
                tables("sigmoid")
                t3 = op("act", lambda e, s=s2, b=bgb: e.activation(s[:, :], b.t[:, :], ACT.Sigmoid), tgb, f2)
                bgb.free = [t3]
                t4 = op("dve", lambda e, s=s2, b=bb: e.tensor_tensor(s[:, :], s[:, :], b.t[:, :], ALU.mult), t3, tb)
                bb.free = [t4]
                t5 = op("dve", lambda e, s=s2, y=y: e.tensor_tensor(y[:, :], y[:, :], s[:, :], ALU.add), t4, t2)
                sg.release(t5)
                tmg = split(y[:, :], mg[0][:, m, :], mg[1][:, m, :], t5)
                mt.release(tmg)
            for m in range(8):
                b, t = dense([(0, wcols("w_out", m * 128, 128))], 8, mg, tmg)
                tx = op("dve", lambda e, b=b, m=m: e.tensor_tensor(xT[:, m, :], b.t[:, :], xT[:, m, :], ALU.add), t)
                b.free = [tx]
                add_square(m, tx)
            P.barrier()
            return tx

        def mixer2():
            place[0] = mark0
            hm = pair([128, 4, 512], "hm")
            at = place[0]
            D = sb([128, 1280], F32, "D")
            S = pair([128, 1280], "S")
            place[0] = at
            ha = pair([128, 4, 512], "ha")
            mark1 = place[0]
            rings(2)
            mv = pair([128, 4, 512], "mv")
            mark2 = place[0]
            ths = norm_x("norm1")

            rows = [sb([4, 512], F32, "row") for _ in range(4)]
            ir, fr, br, mr = rows
            gcol = sb([128, 4, 4], F32, "gcol")
            lam = sb([128, 4], F32, "lam")
            t_on = op("dve", lambda e: e.memset(mr[:, :], 1.0), P.last["dve"])
            b, t = dense([(0, wcols("w_if", 0, 128))], 8, h, parts_ready=ths)
            t1 = op("dve", lambda e, b=b: e.tensor_scalar(ir[:, :], b.t[0:4, :], col("bi")[0:4, :], None, ALU.add), t, t_c)
            t2 = op("dve", lambda e, b=b: e.tensor_copy(fr[:, :], b.t[32:36, :]), t)
            b.free = [t2]
            t2 = op("dve", lambda e: e.tensor_scalar(fr[:, :], fr[:, :], col("bf")[0:4, :], None, ALU.add), t2)
            t3 = op("act", lambda e: e.activation(br[:, :], fr[:, :], ACT.Abs), t2)
            tables("log_exp")
            t3 = op("act", lambda e: e.activation(br[:, :], br[:, :], ACT.Exp, scale=-1.0), t3)
            tables("log_exp")
            t3 = op("act", lambda e: e.activation(br[:, :], br[:, :], ACT.Ln, bias=col("one")[0:4, :]), t3)
            t3 = op("dve", lambda e: e.scalar_tensor_tensor(fr[:, :], fr[:, :], 0.0, br[:, :], ALU.min, ALU.subtract), t3)
            t3 = op("dve", lambda e: e.tensor_tensor_scan(br[:, :], mr[:, :], fr[:, :], 0.0, ALU.mult, ALU.add), t3, t_on)
            tg = op("dve", lambda e: e.tensor_tensor(ir[:, :], ir[:, :], br[:, :], ALU.subtract), t3, t1)
            tG = op("dve", lambda e: e.tensor_tensor_scan(fr[:, :], ir[:, :], ir[:, :], 0.0, ALU.max, ALU.max), tg)
            tM = op("dve", lambda e: e.tensor_tensor(mr[:, :], br[:, :], fr[:, :], ALU.add), tG)
            b = bank()
            for s in range(4):
                t = op("pe", lambda e, s=s, b=b: e.transpose(b.t[:, 4 * s:4 * s + 4], ir[:, 128 * s:128 * s + 128], mat("ident")[0:4, 0:4]), tg, b.free)
            tgc = op("dve", lambda e, b=b: e.tensor_copy(gcol[:, :, :].rearrange("p a b -> p (a b)"), b.t[:, 0:16]), t)
            b.free = [tgc]

            vbanks = banks[0:4]
            t = token_rows(lambda kk: wcols("w_in_2", 1024, 512, 2 * kk, 2), 512, vbanks, h)
            for tt in range(4):
                tmv = split(vbanks[tt].t[:, :], mv[0][:, tt, :], mv[1][:, tt, :], t)
                vbanks[tt].free = [tmv]

            raw = [sb([128, 515], F32, "raw")]
            cv = Ring(2, [128, 512], name="cv")
            mq, mk = [pair([128, 512], "mq") for _ in range(2)], [pair([128, 512], "mk") for _ in range(2)]
            so = [sb([128, 512], F32, "so")] * 2
            em = sb([128, 512], F32, "em")
            tz = [op("dve", lambda e, x=x: e.memset(x[:, 0:3], 0.0), P.last["dve"]) for x in raw]
            qk_t, so_t, rawfree, qkfree, sofree = {}, {}, [[], []], [[], []], [[], []]

            def conv_chunk(m, out, waits, scale):
                x = raw[0]
                b, t = dense([(0, wcols("w_in_2", m * 128, 128))], 8, h)
                t1 = op("act", lambda e: e.activation(x[:, 3:515], b.t[:, :], ACT.Copy), t, tz, rawfree[0])
                b.free = [t1]
                y, f, _ = cv.get()
                t2 = op("dve", lambda e: e.tensor_scalar(y[:, :], x[:, 0:512], col("conv_w", m), col("conv_b", m), ALU.mult, ALU.add), t1, tz, f, t_c)
                for j in range(1, 4):
                    t2 = op("dve", lambda e, j=j: e.scalar_tensor_tensor(y[:, :], x[:, j:j + 512], col("conv_w", 8 * j + m), y[:, :], ALU.mult, ALU.add), t2)
                rawfree[0] = [t2]
                tables("silu")
                t3 = op("act", lambda e: e.activation(y[:, :], y[:, :], ACT.Silu), t2)
                t4 = split(y[:, :], out[0][:, :], out[1][:, :], t3, waits, scale=scale)
                cv.release(t4)
                return t4

            def prepare(hd):
                k = hd % 2
                t1 = conv_chunk(hd, mq[k], qkfree[k], 1.0)
                t2 = conv_chunk(4 + hd, mk[k], qkfree[k], float(128 ** -0.5))
                qk_t[hd] = [t1, t2]

            dfree, sfree, emfree = [], [], []

            def head(hd):
                nonlocal dfree, sfree, emfree
                k = hd % 2
                b, t = dense([(0, wcols("w_in_2", 1536 + hd * 128, 128))], 8, h)
                tables("sigmoid")
                so_t[hd] = op("act", lambda e: e.activation(so[k][:, :], b.t[:, :], ACT.Sigmoid), t, sofree[0])
                b.free = [so_t[hd]]
                bG, bD, bM = bank(), bank(), bank()
                sel = mat(f"sel{hd}")[0:4, :]
                tgb = mm(bG.t[:, :], sel, fr[:, :], True, True, tG, bG.free)
                mm(bD.t[:, :], sel, fr[:, :], True, False, bD.free, skip=True)
                for j in range(4):
                    tdb = mm(bD.t[:, 128 * j:128 * j + 128], rident[:, :], rpos[:, :], False, j == 3, t_rp, skip=True)
                tmb = mm(bM.t[:, :], sel, mr[:, :], True, True, tM, bM.free)
                tables("log_exp")
                t1 = op("act", lambda e: e.activation(em[:, :], bM.t[:, :], ACT.Exp, scale=-1.0), tmb, emfree)
                bM.free = [t1]
                for j in range(4):
                    o, N = REG[j][2], 512 - 128 * j
                    tables("log_exp")
                    t2 = op("act", lambda e, o=o, j=j: e.activation(D[:, o:o + 128], bD.t[:, 128 * j:128 * j + 128], ACT.Exp, bias=gcol[:, j, hd:hd + 1], scale=-1.0), tdb, tgc, dfree)
                bD.free = [t2]
                for j in range(3):
                    o, N = REG[j][2], 512 - 128 * j
                    tables("log_exp")
                    t2 = op("act", lambda e, o=o, j=j, N=N: e.activation(D[:, o + 128:o + N], bG.t[:, 128 * j + 128:512], ACT.Exp, bias=gcol[:, j, hd:hd + 1], scale=-1.0), tgb)
                bG.free = [t2]
                zs = [bank(), bank(), bank()]
                for j in range(4):
                    bk_, off, o = REG[j]
                    N = 512 - 128 * j
                    t3 = mm3(zs[bk_].t[:, off:off + N], [x[:, 128 * j:128 * j + 128] for x in mk[k]], [x[:, 128 * j:512] for x in mq[k]],
                             True, True, qk_t[hd], zs[bk_].free, skip=True)
                qkfree[k] = [t3]
                for bk_, o, n in ((0, 0, 512), (1, 512, 512), (2, 1024, 256)):
                    t4 = op("dve", lambda e, bk_=bk_, o=o, n=n: e.tensor_tensor(D[:, o:o + n], zs[bk_].t[:, 0:n], D[:, o:o + n], ALU.mult), t3, t2)
                for bb in zs:
                    bb.free = [t4]
                t5 = split(D[:, :], S[0][:, :], S[1][:, :], t4, sfree)
                dfree = [t5]
                bn, bd = bank(), bank()
                for j in range(4):
                    o, N = REG[j][2], 512 - 128 * j
                    t6 = mm3(bn.t[:, 128 * j:512], (mv[0][:, j, hd * 128:hd * 128 + 128], mv[1][:, j, hd * 128:hd * 128 + 128]),
                             [x[:, o:o + N] for x in S], j == 0, j == 3, t5, tmv, bn.free)
                for j in range(4):
                    o, N = REG[j][2], 512 - 128 * j
                    for part in S:
                        t7 = mm(bd.t[:, 128 * j:512], rones[:, :], part[:, o:o + N], j == 0 and part is S[0], j == 3 and part is S[1], t_rp, bd.free)
                sfree = [t7]
                a, f, _ = tmp["sq"].get()
                ta = op("act", lambda e: e.activation(a[:, :], bd.t[:, :], ACT.Abs), t7, f)
                bd.free = [ta]
                ta = op("dve", lambda e: e.tensor_tensor(a[:, :], a[:, :], em[:, :], ALU.max), ta, t1)
                emfree = [ta]
                tables("log_exp")
                ta = op("act", lambda e: e.activation(a[:, :], a[:, :], ACT.Ln), ta)
                tables("log_exp")
                ta = op("act", lambda e: e.activation(a[:, :], a[:, :], ACT.Exp, scale=-1.0), ta)
                y, f, _ = tmp["y"].get()
                ty = op("dve", lambda e: e.tensor_tensor(y[:, :], bn.t[:, :], a[:, :], ALU.mult), ta, t6, f)
                bn.free = [ty]
                tmp["sq"].release(ty)
                ty = op("dve", lambda e: e.tensor_tensor(y[:, :], y[:, :], so[k][:, :], ALU.mult), ty, so_t[hd])
                sofree[0] = [ty]
                r, tr = rms(lambda q: y[:, :], 1, mat("mean128"), ty)
                ty = op("dve", lambda e: e.scalar_tensor_tensor(y[:, :], y[:, :], col("m_norm"), r[:, :], ALU.mult, ALU.mult), tr)
                tmp["rr"].release(ty)
                t8 = split(y[:, :], hm[0][:, hd, :], hm[1][:, hd, :], ty)
                tmp["y"].release(t8)
                return t8

            prepare(0)
            for hd in range(4):
                if hd < 3:
                    prepare(hd + 1)
                thm = head(hd)
            P.barrier()

            place[0] = mark2
            av = mv
            lam = sb([128, 4], F32, "lam")
            aq, ak = [pair([128, 512], "aq") for _ in range(2)], [pair([128, 512], "ak") for _ in range(2)]
            p0, p1 = Ring(2, [128, 512], name="p0"), Ring(2, [128, 512], name="p1")
            PT = [pair([128, 1280], "PT")] * 2
            st = sb([128, 16, 4], F32, "st")
            t = op("dve", lambda e: e.tensor_tensor(lam[:, 0:2], cols[:, COLS["lq1"][0]:COLS["lq1"][0] + 2], cols[:, COLS["lk1"][0]:COLS["lk1"][0] + 2], ALU.mult), P.last["dve"])
            b = bank()
            t = mm(b.t[:, 0:2], mat("ones"), lam[:, 0:2], True, True, t, b.free)
            tables("log_exp")
            t = op("act", lambda e, b=b: e.activation(lam[:, 0:2], b.t[:, 0:2], ACT.Exp), t)
            b.free = [t]
            t = op("dve", lambda e: e.tensor_tensor(lam[:, 2:3], lam[:, 1:2], lam[:, 0:1], ALU.subtract), t)
            tl = op("dve", lambda e: e.tensor_scalar(lam[:, 3:4], lam[:, 2:3], 1.0, -(0.8 - 0.6 * 1.0), ALU.mult, ALU.add), t)
            t = token_rows(lambda kk: wcols("w_in_2", 3080, 512, 2 * kk, 2), 512, vbanks, h)
            for tt in range(4):
                tav = split(vbanks[tt].t[:, :], av[0][:, tt, :], av[1][:, tt, :], t)
                vbanks[tt].free = [tav]
            qk2, ptf, ptt = {}, [[], []], {}
            qkf = [[], []]

            def prepare2(hd):
                k = hd % 2
                for f in qkf[k]:
                    f.used = True
                b, t = dense([(0, wcols("w_in_2", 2056 + hd * 128, 128))], 8, h)
                t1 = chunk_norm(b, t, mat("blk64"), col("q_norm"), (aq[k][0][:, :], aq[k][1][:, :]), scale=0.125, before=qkf[k])
                b, t = dense([(0, wcols("w_in_2", 2568 + hd * 128, 128))], 8, h)
                t2 = chunk_norm(b, t, mat("blk64"), col("k_norm"), (ak[k][0][:, :], ak[k][1][:, :]), before=qkf[k])
                qk2[hd] = [t1, t2]

            ready = {}

            def first(n):
                hd, i = n // 4, n % 4
                k, W = hd % 2, 128 * (i + 1)
                ps = []
                for c in range(2):
                    po = 64 * c
                    b = bank()
                    mm3(b.t[:, 0:W], [x[po:po + 64, 128 * i:128 * i + 128] for x in aq[k]], [x[po:po + 64, 0:W] for x in ak[k]],
                        True, False, qk2[hd], b.free)
                    t = mm(b.t[:, 128 * i:W], rident[:, :], rdm[:, :], False, True, t_rp)
                    p, f, _ = (p0, p1)[c].get()
                    t1 = op("dve", lambda e, b=b, c=c: e.tensor_reduce(st[:, n, c:c + 1], b.t[:, 0:W], AX.X, ALU.max, negate=True), t)
                    tables("log_exp")
                    t2 = op("act", lambda e, b=b, c=c, p=p: e.activation(p[:, 0:W], b.t[:, 0:W], ACT.Exp, bias=st[:, n, c:c + 1], accum_out=st[:, n, 2 + c:3 + c]), t1, f)
                    b.free = [t2]
                    ps.append((p, t2))
                qkf[k] = [t]
                t3 = op("dve", lambda e: e.reciprocal(st[:, n, 2:4], st[:, n, 2:4]), ps[0][1], ps[1][1])
                t4 = op("dve", lambda e: e.tensor_scalar(st[:, n, 3:4], st[:, n, 3:4], lam[:, 3:4], None, ALU.mult), t3, tl)
                a, bb = ps[0][0], ps[1][0]
                t5 = op("dve", lambda e: e.tensor_scalar(a[:, 0:W], a[:, 0:W], st[:, n, 2:3], None, ALU.mult), t3)
                t6 = op("dve", lambda e: e.scalar_tensor_tensor(a[:, 0:W], bb[:, 0:W], st[:, n, 3:4], a[:, 0:W], ALU.mult, ALU.add), t4, t5)
                p1.free[n % 2] = [t6]
                ready[n] = (a, t6)

            def second(n):
                hd, i = n // 4, n % 4
                a, t = ready.pop(n)
                b = bank()
                for s in range(i + 1):
                    t1 = op("pe", lambda e, s=s, b=b: e.transpose(b.t[:, s * 128:(s + 1) * 128], a[:, s * 128:(s + 1) * 128], mat("ident")), t, b.free)
                p0.free[n % 2] = [t1]
                k = hd % 2
                for s in range(i + 1):
                    o = REG[s][2] + 128 * (i - s)
                    t2 = op("act", lambda e, s=s, b=b, o=o: e.activation(PT[k][0][:, o:o + 128], b.t[:, s * 128:(s + 1) * 128], ACT.Copy), t1, ptf[0])
                for s in range(i + 1):
                    o = REG[s][2] + 128 * (i - s)
                    t3 = op("dve", lambda e, s=s, b=b, o=o: e.tensor_tensor(PT[k][1][:, o:o + 128], b.t[:, s * 128:(s + 1) * 128], PT[k][0][:, o:o + 128].bitcast(F32), ALU.subtract), t2, ptf[0])
                b.free = [t3]
                if i < 3:
                    return
                b2 = bank()
                for j in range(4):
                    o, N = REG[j][2], 512 - 128 * j
                    t4 = mm3(b2.t[:, 128 * j:512], (av[0][:, j, hd * 128:hd * 128 + 128], av[1][:, j, hd * 128:hd * 128 + 128]),
                             [x[:, o:o + N] for x in PT[k]], j == 0, j == 3, t3, tav, b2.free)
                ptf[0] = [t4]
                y, f, _ = tmp["y"].get()
                ty = op("act", lambda e: e.activation(y[:, :], b2.t[:, :], ACT.Copy), t4, f)
                b2.free = [ty]
                r, tr = rms(lambda q: y[:, :], 1, mat("mean128"), ty)
                ty = op("dve", lambda e: e.scalar_tensor_tensor(y[:, :], y[:, :], col("a_norm"), r[:, :], ALU.mult, ALU.mult), tr)
                tmp["rr"].release(ty)
                t8 = split(y[:, :], ha[0][:, hd, :], ha[1][:, hd, :], ty, scale=1.0 - (0.8 - 0.6 * 1.0))
                tmp["y"].release(t8)
                return t8

            prepare2(0)
            for n in range(17):
                if n < 16:
                    if n % 4 == 0 and n // 4 < 3:
                        prepare2(n // 4 + 1)
                    first(n)
                if n >= 1:
                    tha = second(n - 1)
            for m in range(8):
                u = use([(0, wcols("w_out_2", m * 128, 128))], 8, 128)
                b = bank()
                for k in range(8):
                    src = (hm, ha)[k // 4]
                    t = mm3(b.t[:, :], (u.H[:, k, :], u.L[:, k, :]), (src[0][:, k % 4, :], src[1][:, k % 4, :]), k == 0, k == 7,
                            u.t_lo, u.t_hi, b.free, thm, tha)
                u.done = t
                tx = op("dve", lambda e, b=b, m=m: e.tensor_tensor(xT[:, m, :], b.t[:, :], xT[:, m, :], ALU.add), t)
                b.free = [tx]
            P.barrier()
            return tx

        def moe():
            place[0] = mark0
            xt = sb([128, 4, 1024], F32, "xt")
            di = [sb([128, 4], I32, "di") for _ in range(2)]
            ei = sb([128, 8], I32, "ei")
            rt = {k: sb([128, 4], F32, k) for k in ("w1", "w2")}
            mark3 = place[0]
            moe_top = top_end
            more = []
            while moe_top - 4096 >= mark3 + 32768 and len(more) < 12:
                moe_top -= 4096
                more.append(Slot(nc.alloc_sbuf_tensor_at(f"stage_moe{len(more)}", [128, 1024], F32, offset=moe_top)))
                more[-1].after = [P.last[e] for e in ("pe", "act", "dve")]
            stream["stage"] += more
            n2 = sb([128, 1024], F32, "n2")
            hb = [sb([128, 1024], F32, "hb") for _ in range(4)]
            wr = pair([128, 8, 36], "wr")
            wrF = sb([128, 8, 36], F32, "wrF")
            br = sb([128, 36], F32, "br")
            rt |= {k: sb([128] + s, F32, k) for k, s in
                  dict(lg=[4, 36], gm=[4], a4=[4, 4], oh=[4, 4], em=[4, 32], a32=[4, 32], o1=[4, 32], o2=[4, 32],
                       v1=[4], v2=[4], gw=[4], vm=[4], ct=[32], nx=[32], cx=[32], on=[32], ps=[4, 32],
                       dx=[32], d1=[4], d2=[4], ss=[4], rs=[4], ei=[8]).items()}
            tn = load(n2[:, :], A["norm2"].partition_broadcast(128).rearrange("p a n -> p (a n)"), P.last["dve"], P.last["pe"], P.last["act"])
            tbr = load(br[:, :], A["b_r"].partition_broadcast(128).rearrange("p a n -> p (a n)"))
            twr = load(wrF[:, :, :], wcols("w_r", 0, 36))
            twr = split(wrF[:, :, :], wr[0][:, :, :], wr[1][:, :, :], twr)
            ext = mats[:, MATS.index("extra"), :]
            s_sc = sem("s_sc")
            for tt in range(4):
                for q in range(2):
                    b = bank()
                    for k in range(4):
                        t = op("pe", lambda e, k=k, q=q, tt=tt, b=b: e.transpose(b.t[:, k * 128:(k + 1) * 128], xT[:, 4 * q + k, tt * 128:(tt + 1) * 128], mat("ident")), b.free)
                    t1 = op("dve" if q else "act", (lambda e, q=q, tt=tt, b=b: e.tensor_copy(xt[:, tt, 512 * q:512 * q + 512], b.t[:, :])) if q
                            else (lambda e, q=q, tt=tt, b=b: e.activation(xt[:, tt, 512 * q:512 * q + 512], b.t[:, :], ACT.Copy)), t)
                    b.free = [t1]
                    if q == 0:
                        t0 = t1
                hb_, x_ = hb[tt], xt[:, tt, :]
                t2 = op("act", lambda e, hb_=hb_, x_=x_, tt=tt: e.activation(hb_[:, :], x_, ACT.Square, accum_out=rt["ss"][:, tt:tt + 1]), t0, t1)
                t2 = op("dve", lambda e, tt=tt: e.tensor_scalar(rt["rs"][:, tt:tt + 1], rt["ss"][:, tt:tt + 1], 1.0 / 1024, EPS, ALU.mult, ALU.add), t2)
                tables("log_exp")
                t2 = op("act", lambda e, tt=tt: e.activation(rt["rs"][:, tt:tt + 1], rt["rs"][:, tt:tt + 1], ACT.Ln), t2)
                tables("log_exp")
                t2 = op("act", lambda e, tt=tt: e.activation(rt["rs"][:, tt:tt + 1], rt["rs"][:, tt:tt + 1], ACT.Exp, scale=-0.5), t2)
                t2 = op("dve", lambda e, hb_=hb_, x_=x_, tt=tt: e.scalar_tensor_tensor(hb_[:, :], x_, rt["rs"][:, tt:tt + 1], n2[:, :], ALU.mult, ALU.mult), t2, tn)
                for q in range(2):
                    b = bank()
                    for k in range(4):
                        t = op("pe", lambda e, k=k, q=q, b=b, hb_=hb_: e.transpose(b.t[:, k * 128:(k + 1) * 128], hb_[:, (4 * q + k) * 128:(4 * q + k + 1) * 128], mat("ident")), t2, b.free)
                    t3 = split(b.t[:, :].rearrange("p (k n) -> p k n", k=4), hH[:, 4 * q:4 * q + 4, tt * 128:(tt + 1) * 128],
                               hL[:, 4 * q:4 * q + 4, tt * 128:(tt + 1) * 128], t)
                    b.free = [t3]
            b = bank()
            for tt in range(4):
                for k in range(8):
                    t = mm3(b.t[:, 36 * tt:36 * tt + 36], [x[:, k, tt * 128:(tt + 1) * 128] for x in h], [x[:, k, :] for x in wr],
                            k == 0, k == 7, t3, twr, b.free, skip=True)
            R = rt

            def v(fn, *w):
                return op("dve", fn, P.last["dve"], *w)

            def bc(ap, shape, axis=2):
                return ap.unsqueeze(axis).broadcast_to(shape)

            v(lambda e, b=b: e.tensor_tensor(R["lg"][:, :, :], b.t[:, 0:144].rearrange("p (a n) -> p a n", a=4), bc(br[:, :], [128, 4, 36], 1), ALU.add), t, tbr)
            b.free = [P.last["dve"]]
            G = R["lg"][:, :, 0:4]
            E4 = R["lg"][:, :, 4:36].rearrange("p a (g n) -> p a g n", g=4)
            v(lambda e: e.tensor_reduce(R["gm"][:, :], G, AX.X, ALU.max))
            v(lambda e: e.tensor_tensor(R["a4"][:, :, :], G, bc(R["gm"][:, :], [128, 4, 4]), ALU.subtract))
            v(lambda e: e.tensor_tensor(R["oh"][:, :, :], G, bc(R["gm"][:, :], [128, 4, 4]), ALU.is_equal))
            v(lambda e: e.tensor_tensor(R["oh"][:, :, :], R["oh"][:, :, :], bc(ext[:, 32:36], [128, 4, 4], 1), ALU.mult))
            v(lambda e: e.tensor_reduce(R["vm"][:, :], R["oh"][:, :, :], AX.X, ALU.max))
            v(lambda e: e.tensor_tensor(R["oh"][:, :, :], R["oh"][:, :, :], bc(R["vm"][:, :], [128, 4, 4]), ALU.is_equal))
            tables("log_exp")
            tt1 = op("act", lambda e: e.activation(R["a4"][:, :, :], R["a4"][:, :, :], ACT.Exp), P.last["dve"])
            v(lambda e: e.tensor_reduce(R["gw"][:, :], R["a4"][:, :, :], AX.X, ALU.add), tt1)
            v(lambda e: e.reciprocal(R["gw"][:, :], R["gw"][:, :]))
            v(lambda e: e.tensor_scalar(R["oh"][:, :, :], R["oh"][:, :, :], -NEG, NEG, ALU.mult, ALU.add))
            EM = R["em"][:, :, :].rearrange("p a (g n) -> p a g n", g=4)
            for g_ in range(4):
                v(lambda e, g_=g_: e.tensor_tensor(EM[:, :, g_, :], E4[:, :, g_, :], bc(R["oh"][:, :, g_], [128, 4, 8]), ALU.add))
            for o_, v_ in (("o1", "v1"), ("o2", "v2")):
                v(lambda e, v_=v_: e.tensor_reduce(R[v_][:, :], R["em"][:, :, :], AX.X, ALU.max))
                v(lambda e, v_=v_: e.tensor_tensor(R["a32"][:, :, :], R["em"][:, :, :], bc(R[v_][:, :], [128, 4, 32]), ALU.is_equal))
                v(lambda e: e.tensor_tensor(R["a32"][:, :, :], R["a32"][:, :, :], bc(ext[:, 36:68], [128, 4, 32], 1), ALU.mult))
                v(lambda e: e.tensor_reduce(R["vm"][:, :], R["a32"][:, :, :], AX.X, ALU.max))
                v(lambda e, o_=o_: e.tensor_tensor(R[o_][:, :, :], R["a32"][:, :, :], bc(R["vm"][:, :], [128, 4, 32]), ALU.is_equal))
                if o_ == "o1":
                    v(lambda e: e.scalar_tensor_tensor(R["em"][:, :, :], R["o1"][:, :, :], 2 * NEG, R["em"][:, :, :], ALU.mult, ALU.add))
            v(lambda e: e.tensor_tensor(R["v2"][:, :], R["v2"][:, :], R["v1"][:, :], ALU.subtract))
            tables("log_exp")
            tt1 = op("act", lambda e: e.activation(R["v2"][:, :], R["v2"][:, :], ACT.Exp), P.last["dve"])
            v(lambda e: e.tensor_scalar(R["w1"][:, :], R["v2"][:, :], 1.0, None, ALU.add), tt1)
            v(lambda e: e.reciprocal(R["w1"][:, :], R["w1"][:, :]))
            v(lambda e: e.tensor_tensor(R["w1"][:, :], R["w1"][:, :], R["gw"][:, :], ALU.mult))
            v(lambda e: e.tensor_tensor(R["w2"][:, :], R["w1"][:, :], R["v2"][:, :], ALU.mult))
            ta = v(lambda e: e.tensor_tensor(R["a32"][:, :, :], R["o1"][:, :, :], R["o2"][:, :, :], ALU.add))
            b, b2 = bank(), bank()
            for tt in range(4):
                for t2_ in range(tt + 1):
                    t = mm(b.t[:, 32 * tt:32 * tt + 32], mat("tru") if t2_ == tt else mat("ones"), R["a32"][:, t2_, :], t2_ == 0, t2_ == tt, ta, b.free, skip=True)
                t = mm(b2.t[:, 0:32], mat("ones"), R["a32"][:, tt, :], tt == 0, tt == 3, b2.free)
            v(lambda e, b=b: e.tensor_copy(R["ps"][:, :, :].rearrange("p a n -> p (a n)"), b.t[:, 0:128]), t)
            b.free = [P.last["dve"]]
            v(lambda e, b=b2: e.tensor_copy(R["ct"][:, :], b.t[:, 0:32]))
            b2.free = [P.last["dve"]]
            v(lambda e: e.tensor_scalar(R["nx"][:, :], R["ct"][:, :], 128.0, None, ALU.is_gt))
            for c in (256.0, 384.0):
                v(lambda e, c=c: e.scalar_tensor_tensor(R["nx"][:, :], R["ct"][:, :], c, R["nx"][:, :], ALU.is_gt, ALU.add))
            v(lambda e: e.memset(R["on"][:, :], 1.0))
            v(lambda e: e.tensor_tensor_scan(R["cx"][:, :], R["on"][:, :], R["nx"][:, :], 0.0, ALU.mult, ALU.add))
            for x in range(NX):
                v(lambda e, x=x: e.tensor_scalar(R["dx"][:, :], R["cx"][:, :], float(x), None, ALU.is_le))
                v(lambda e, x=x: e.tensor_reduce(R["ei"][:, x:x + 1], R["dx"][:, :], AX.X, ALU.add))
            v(lambda e: e.tensor_copy(R["ei"][:, 7:8], R["cx"][:, 31:32]))
            v(lambda e: e.tensor_scalar(R["ei"][:, 0:7], R["ei"][:, 0:7], 31.0, None, ALU.min))
            v(lambda e: e.tensor_copy(ei[:, :], R["ei"][:, :]))
            v(lambda e: e.tensor_tensor(R["dx"][:, :], R["cx"][:, :], R["nx"][:, :], ALU.subtract))
            v(lambda e: e.tensor_scalar(R["dx"][:, :], R["dx"][:, :], 128.0, 128.0 * (NB - 1), ALU.mult, ALU.add))
            v(lambda e: e.tensor_tensor(R["dx"][:, :], R["dx"][:, :], ext[:, 0:32], ALU.subtract))
            v(lambda e: e.tensor_scalar(R["a32"][:, :, :], R["ps"][:, :, :], 128.0, None, ALU.is_ge))
            v(lambda e: e.tensor_tensor(R["a32"][:, :, :], R["a32"][:, :, :], bc(R["dx"][:, :], [128, 4, 32], 1), ALU.mult))
            v(lambda e: e.tensor_tensor(R["ps"][:, :, :], R["ps"][:, :, :], R["a32"][:, :, :], ALU.add))
            v(lambda e: e.tensor_tensor(R["ps"][:, :, :], R["ps"][:, :, :], bc(ext[:, 0:32], [128, 4, 32], 1), ALU.add))
            for q, o_ in enumerate(("o1", "o2")):
                v(lambda e, o_=o_: e.tensor_tensor(R["a32"][:, :, :], R["ps"][:, :, :], R[o_][:, :, :], ALU.mult))
                v(lambda e: e.tensor_reduce(R["d1"][:, :], R["a32"][:, :, :], AX.X, ALU.add))
                v(lambda e, q=q: e.tensor_copy(di[q][:, :], R["d1"][:, :]))
            tdi = P.last["dve"]

            for tt in range(4):
                for q in range(2):
                    tsc = dma("pool", lambda e, tt=tt, q=q: e.indirect_dma_start(
                        out=xb_d[:, :], out_offset=bass.IndirectOffsetOnAxis(ap=di[q][:, tt:tt + 1], axis=0),
                        in_=hb[tt][:, :], in_offset=None).then_inc(s_sc, 16), s_sc, tdi, t_zero[-1])
            P.barrier(also=[tsc])

            place[0] = mark3
            for k in range(3):
                stream["split"].append(Slot(*pair([128, 1024], "w_moe")))
                stream["split"][-1].after = [P.last[e] for e in ("pe", "act", "dve")] + [tsc]
            stream["ahead"] = 4
            place[0] = x_place
            NGR = 3
            xg = [sb([128, 1024], F32, "xg") for _ in range(NGR)]
            s_xg = [sem("s_xg") for _ in range(NGR)]
            xgT = [pair([128, 8, 128], "xgT") for _ in range(2)]
            hid = [sb([128, 512], F32, "hid") for _ in range(2)]
            hT = [pair([128, 4, 128], "hT") for _ in range(2)]
            yo = [sb([128, 1024], F32, "yo") for _ in range(2)]
            assert place[0] <= x_place + 49152
            s_yo = [sem("s_yo") for _ in range(2)]
            F = dict(xg=[[] for _ in range(NGR)], xgT=[[], []], hid=[[], []], hT=[[], []], yo=[[], []])
            xg_t, xT_t = {}, {}

            def fetch(n, *waits):
                k = n % NGR
                xg_t[n] = dma("pool", lambda e: e.dma_start(xg[k][:, :], xb_d[n * 128:(n + 1) * 128, :]).then_inc(s_xg[k], 16), s_xg[k], F["xg"][k], *waits)

            def turn_x(n):
                k = n % NGR
                for q in range(2):
                    b = bank()
                    for j in range(4):
                        t = op("pe", lambda e, j=j, q=q, b=b: e.transpose(b.t[:, j * 128:(j + 1) * 128], xg[k][:, (4 * q + j) * 128:(4 * q + j + 1) * 128], mat("ident")), xg_t[n], b.free)
                    t1 = split(b.t[:, :].rearrange("p (k n) -> p k n", k=4), xgT[n % 2][0][:, 4 * q:4 * q + 4, :], xgT[n % 2][1][:, 4 * q:4 * q + 4, :], t, F["xgT"][n % 2])
                    b.free = [t1]
                F["xg"][k] = [t]
                xT_t[n] = t1

            def block_(n, wsrc, ahead=True, nxt=None):
                x = xgT[n % 2]
                bs = []
                for name in ("w_gate_2", "w_up_2"):
                    b = bank()
                    for kk in range(4):
                        u = use([(0, wsrc(name, 2 * kk, 2))], 2, 512, ahead=ahead)
                        for j in range(2):
                            t = mm3(b.t[:, :], [y[:, 2 * kk + j, :] for y in x], (u.H[:, j, :], u.L[:, j, :]),
                                    kk == 0 and j == 0, kk == 3 and j == 1, u.t_lo, u.t_hi, b.free, xT_t[n])
                        u.done = t
                    bs.append((b, t))
                F["xgT"][n % 2] = [t]
                hd_ = hid[n % 2]
                (bg, tg_), (bu, tu_) = bs
                tables("silu")
                t1 = op("act", lambda e: e.activation(hd_[:, :], bg.t[:, :], ACT.Silu), tg_, F["hid"][n % 2])
                bg.free = [t1]
                t2 = op("dve", lambda e: e.tensor_tensor(hd_[:, :], hd_[:, :], bu.t[:, :], ALU.mult), t1, tu_)
                bu.free = [t2]
                if nxt is not None:
                    turn_x(nxt)
                b = bank()
                for j in range(4):
                    t3 = op("pe", lambda e, j=j, b=b: e.transpose(b.t[:, j * 128:(j + 1) * 128], hd_[:, j * 128:(j + 1) * 128], mat("ident")), t2, b.free)
                F["hid"][n % 2] = [t3]
                hh = hT[n % 2]
                t4 = split(b.t[:, :].rearrange("p (k n) -> p k n", k=4), hh[0][:, :, :], hh[1][:, :, :], t3, F["hT"][n % 2])
                b.free = [t4]
                ob = [bank(), bank()]
                for j in range(4):
                    u = use([(0, wsrc("w_down_2", j, 1))], 1, 1024, ahead=ahead)
                    for c in range(2):
                        t = mm3(ob[c].t[:, :], (hh[0][:, j, :], hh[1][:, j, :]), (u.H[:, 0, 512 * c:512 * c + 512], u.L[:, 0, 512 * c:512 * c + 512]),
                                j == 0, j == 3, u.t_lo, u.t_hi, ob[c].free, t4)
                    u.done = t
                F["hT"][n % 2] = [t]
                o = yo[n % 2]
                t1 = op("act", lambda e: e.activation(o[:, 0:512], ob[0].t[:, :], ACT.Copy), t, F["yo"][n % 2])
                t2 = op("act", lambda e: e.activation(o[:, 512:1024], ob[1].t[:, :], ACT.Copy))
                ob[0].free, ob[1].free = [t1], [t2]
                k = n % 2
                ts = dma("pool", lambda e: e.dma_start(yb_d[n * 128:(n + 1) * 128, :], o[:, :]).then_inc(s_yo[k], 16), s_yo[k], t1, t2)
                F["yo"][k] = [ts]
                return ts

            for n in range(NGR):
                fetch(n)
            turn_x(0)
            for n in range(NB):
                ts = block_(n, lambda name, k, c, n=n: A[name][n].rearrange("(k p) n -> p k n", p=128)[:, k:k + c, :],
                            nxt=n + 1 if n + 1 < NB else None)
                if n + NGR < NB:
                    fetch(n + NGR)
            stores = [F["yo"][0], F["yo"][1]]
            P.barrier(engs=("pe", "act", "dve", "pool", "sp"), also=stores[0] + stores[1])

            for x in range(NX):
                P.region_begin()
                F.update(xg=[[] for _ in range(NGR)], xgT=[[], []], hid=[[], []], hT=[[], []], yo=[[], []])
                for bb in banks:
                    bb.free = []
                for uu in units:
                    uu.t_lo = uu.t_hi = uu.done = None
                del holes[len(units):]
                n = NB + x
                fetch(n)
                turn_x(n)

                def wdyn(name, k, c, x=x):
                    def src(e):
                        r = P.regs[x]
                        w = A[name].rearrange("e (k p) n -> e p k n", p=128)
                        return w[bass.ds(r, 1), :, k:k + c, :].rearrange("e p k n -> (e p) k n")
                    return src
                ts = block_(n, wdyn, ahead=False)
                P.barrier(also=[ts], engs=("pe", "act", "dve", "pool", "sp"))
                P.region_end(x)

            place[0] = x_place
            y1 = [sb([128, 1024], F32, "y1") for _ in range(2)]
            y2 = [sb([128, 1024], F32, "y2") for _ in range(2)]
            s_g = [sem("s_g") for _ in range(4)]
            s_out = sem("s_out")
            free = [[], []]
            for tt in range(4):
                k = tt % 2
                tg_ = []
                for q, yy in ((0, y1), (1, y2)):
                    s = s_g[2 * k + q]
                    tg_.append(dma("pool", lambda e, tt=tt, q=q, yy=yy, k=k, s=s: e.indirect_dma_start(
                        out=yy[k][:, :], out_offset=None, in_=yb_d[:, :],
                        in_offset=bass.IndirectOffsetOnAxis(ap=di[q][:, tt:tt + 1], axis=0)).then_inc(s, 16), s, free[k]))
                t1 = op("dve", lambda e, k=k, tt=tt: e.tensor_scalar(y1[k][:, :], y1[k][:, :], R["w1"][:, tt:tt + 1], None, ALU.mult), tg_[0])
                t1 = op("dve", lambda e, k=k, tt=tt: e.scalar_tensor_tensor(y1[k][:, :], y2[k][:, :], R["w2"][:, tt:tt + 1], y1[k][:, :], ALU.mult, ALU.add), t1, tg_[1])
                t1 = op("dve", lambda e, k=k, tt=tt: e.tensor_tensor(xt[:, tt, :], xt[:, tt, :], y1[k][:, :], ALU.add), t1)
                free[k] = [t1]
                tend = dma("act", lambda e, tt=tt: e.dma_start(out[tt * 128:(tt + 1) * 128, :], xt[:, tt, :]).then_inc(s_out, 16), s_out, t1)
            P.q["act"].append([None, [tend], None])
            P.ei = ei


        h = (hH, hL)
        for k in range(8):
            add_square(k, t_c)
        tx = ffn("w1_gate", "w1_up", "w1_down", "g_ffn1")
        tx = mixer1()
        tx = ffn("w2_gate", "w2_up", "w2_down", "g_ffn2")
        tx = mixer2()
        moe()
        block = ctx.enter_context(nc.Block())
        P.emit(block)


def _layout(inputs):
    f = {k: np.asarray(v) for k, v in inputs.items()}

    def chunks(v):
        return v.reshape(-1, 128).T

    def twice(v):
        return np.concatenate([v.reshape(-1), v.reshape(-1)])[:, None]

    def padded(v, n=128):
        v = v.reshape(-1)
        return np.concatenate([v, np.zeros(n - v.size, np.float32)])[:, None]

    inv = (np.float32(10000.0) ** (-np.arange(0, 64, 2, dtype=np.float32) / np.float32(64))).astype(np.float32)
    p = {
        "g_ffn1": chunks(f["g_ffn1"]), "g_mix": chunks(f["g_mix"]), "g_cq": chunks(f["g_cq"]),
        "g_q_a": twice(f["g_q_a"]), "g_k_a": twice(f["g_k_a"]), "g_ffn2": chunks(f["g_ffn2"]),
        "norm1": chunks(f["norm1_w_2"]), "conv_w": np.concatenate([chunks(f["conv_w_2"][0, j]) for j in range(4)], axis=1),
        "conv_b": chunks(f["conv_b_2"]), "m_norm": chunks(f["m_norm_w_2"]), "q_norm": twice(f["q_norm_w_2"]),
        "k_norm": twice(f["k_norm_w_2"]), "a_norm": chunks(f["a_norm_w_2"]), "bi": padded(f["b_igate_2"]),
        "bf": padded(f["b_fgate_2"]), "lq1": padded(f["lambda_q1_2"]), "lq2": padded(f["lambda_q2_2"]),
        "lk1": padded(f["lambda_k1_2"]), "lk2": padded(f["lambda_k2_2"]),
        "inv_freq": np.tile(inv, 4)[:, None], "sgn": np.tile(np.repeat(np.array([-1.0, 1.0], np.float32), 32), 2)[:, None],
        "eps": np.full((128, 1), EPS, np.float32), "one": np.ones((128, 1), np.float32),
    }
    a = {"cols": np.concatenate([p[k].reshape(128, -1) for k in COLS], axis=1), "mats": shape_constants()}
    a["x"] = f["x"][0].T.reshape(8, 128, 512).transpose(1, 0, 2)
    a["positions"] = f["positions"]
    w, w2 = f["w_in"][0], f["w_in_2"][0]
    for k in ("w1_gate", "w1_up", "w1_down", "w2_gate", "w2_up", "w2_down", "w_in", "w_o_a", "w_o_b", "w_out", "w_uq_a",
              "w_q_idx", "w_uv_a", "w_in_2", "w_out_2", "w_gate_2", "w_up_2", "w_down_2"):
        a[k] = f[k][0]
    a["w_k2"] = np.concatenate([w[:, 256:320], w[:, 256:320], w[:, 448:512], w[:, 448:512]], axis=1)
    a["w_vw"] = np.concatenate([w[:, 320:448], w[:, 512:520]], axis=1)
    gap = np.zeros((1024, 28), np.float32)
    a["w_if"] = np.concatenate([w2[:, 2048:2052], gap, w2[:, 2052:2056], gap, gap, gap, gap[:, 0:8]], axis=1)
    a["w_r"] = np.concatenate([f["w_group_2"][0], f["w_expert_2"][0]], axis=1)
    a["b_r"] = np.concatenate([f["b_group_2"], f["b_expert_2"]], axis=1)
    a["norm2"] = f["norm2_w_2"]
    return {k: np.ascontiguousarray(v) for k, v in a.items()}


def kernel(**inputs):
    import numpy as _np
    import concourse.bacc as _bacc
    from concourse import mybir as _mybir
    from concourse.bass_utils import run_bass_kernel_spmd as _run

    nc = _bacc.Bacc("TRN2", target_bir_lowering=False, num_devices=1)
    arrays = _layout(inputs)
    handles = {k: nc.dram_tensor(k, v.shape, _mybir.dt.from_np(v.dtype), kind="ExternalInput").ap() for k, v in arrays.items()}
    out = nc.dram_tensor("out", (512, 1024), _mybir.dt.float32, kind="ExternalOutput").ap()
    build(nc, handles, out)
    r = _run(nc, [arrays], core_ids=[0])
    return _np.asarray(r.results[0]["out"]).reshape(1, 512, 1024)
```

```python
import numpy as np
import concourse.bass as bass
from concourse import mybir

F32 = mybir.dt.float32
F32R = mybir.dt.float32r
I32 = mybir.dt.int32
ALU = mybir.AluOpType
ACT = mybir.ActivationFunctionType
AX = mybir.AxisListType

NEG = -1.0e30
REPL = -3.0e38
EPS = 1e-6
CAP = 1408
NSTAGE, NSPLIT, AHEAD = 4, 3, 2
NB = 32
BLK = 64
NX = 15
NSLOT = (NB + NX) * BLK

COLS = {}


def _cols():
    at = 0
    for name, n in [("g_ffn1", 8), ("g_mix", 8), ("g_cq", 2), ("g_q_a", 1), ("g_k_a", 1), ("g_ffn2", 8),
                    ("norm1", 8), ("conv_w", 32), ("conv_b", 8), ("m_norm", 1), ("q_norm", 1), ("k_norm", 1),
                    ("a_norm", 1), ("bi", 1), ("bf", 1), ("lq1", 1), ("lq2", 1), ("lk1", 1), ("lk2", 1),
                    ("inv_freq", 1), ("sgn", 1), ("norm2", 8), ("b_r", 1), ("eps", 1), ("one", 1)]:
        COLS[name] = (at, n)
        at += n
    return at


NCOLS = _cols()
MATS = ["ident", "ones", "blk64", "perm", "tru", "extra"]
RMATS = ["ntri", "nones", "mstrict", "mpos", "dmask", "tru"]


def shape_constants():
    i = np.arange(128)
    r, c = i[:, None], i[None, :]
    m = {}
    m["ident"] = r == c
    m["ones"] = np.ones((128, 128))
    m["blk64"] = (r // 64) == (c // 64)
    m["perm"] = r == np.where(c % 64 < 32, c + 32, c - 32)
    m["ntri"] = -(r >= c).astype(np.float32)
    m["nones"] = -np.ones((128, 128))
    m["mstrict"] = np.where(c > r, 0.0, NEG)
    m["mpos"] = np.where(c < r, -NEG, 0.0)
    m["tru"] = r < c
    m["dmask"] = np.where(c // 64 <= r // 64, 0.0, NEG)
    x = np.zeros((128, 128), np.float32)
    x[:, 0:32] = np.arange(32) * float(BLK)
    x[:, 32:36] = 4.0 - np.arange(4)
    x[:, 36:68] = 32.0 - np.arange(32)
    x[:, 68:68 + NX] = np.arange(NX)
    m["extra"] = x
    return np.stack([np.asarray(m[k], np.float32) for k in MATS + RMATS], axis=1).reshape(128, -1)


class Tok:

    def __init__(self, eng, sem=None, val=None):
        self.eng, self.sem, self.val, self.used = eng, sem, val, sem is not None


class Program:

    def __init__(self, nc, ctx):
        self.nc, self.ctx = nc, ctx
        self.q = {e: [] for e in ("pe", "act", "dve", "pool", "sp")}
        self.sem = {e: ctx.enter_context(nc.semaphore("s_" + e)) for e in self.q}
        self.counts = {}
        self.last = {}
        self.main = None
        self.regs = {}
        self.ei = None
        self.tables = None

    def op(self, eng, fn, *waits):
        t = Tok(eng)
        flat = []
        for w in waits:
            flat += [x for x in (w if isinstance(w, (list, tuple)) else [w]) if x is not None]
        for w in flat:
            w.used = True
        self.q[eng].append([fn, flat, t])
        self.last[eng] = t
        return t

    def dma(self, eng, fn, sem, *waits, n=1):
        self.counts[sem] = self.counts.get(sem, 0) + 16 * n
        flat = []
        for w in waits:
            flat += [x for x in (w if isinstance(w, (list, tuple)) else [w]) if x is not None]
        for w in flat:
            w.used = True
        self.q[eng].append([fn, flat, None])
        return Tok("dma", sem, self.counts[sem])

    def hold(self, eng):
        item = [None, [], None]
        self.q[eng].append(item)
        return item

    def barrier(self, engs=("pe", "act", "dve", "pool"), also=()):
        toks = [self.last[e] for e in engs if e in self.last]
        for e in engs:
            ts = [t for t in toks if t.eng != e or e != "pe"] + list(also)
            for t in ts:
                t.used = True
            self.q[e].append([None, ts, None])

    def region_begin(self):
        self.main = (self.q, self.last)
        self.q, self.last = {e: [] for e in self.q}, {}
        self.tables = None

    def region_end(self, n):
        inner = self.q
        self.q, self.last = self.main
        self.main = self.tables = None
        for e in self.q:
            self.q[e].append(("region", inner[e], n))

    def emit(self, block):
        inner = {e: self.ctx.enter_context(self.nc.semaphore("x_" + e)) for e in self.q}
        for e, items in self.q.items():
            n = m = 0
            for it in items:
                if it[0] == "region":
                    for fn, waits, tok in it[1]:
                        if tok is not None and tok.used:
                            m += 1
                            tok.sem, tok.val = inner[e], m
                elif it[2] is not None and it[2].used:
                    n += 1
                    it[2].sem, it[2].val = self.sem[e], n
        for e, deco in (("pe", block.tensor), ("act", block.scalar), ("dve", block.vector),
                        ("pool", block.gpsimd), ("sp", block.sync)):
            def body(eng, e=e):
                seen = {}

                def run(items):
                    for fn, waits, tok in items:
                        for w in waits:
                            if w.eng == e and e == "pe":
                                continue
                            if seen.get(id(w.sem), 0) < w.val:
                                seen[id(w.sem)] = w.val
                                eng.wait_ge(w.sem, w.val)
                        if fn is not None:
                            ins = fn(eng)
                            if tok is not None and tok.used:
                                ins.then_inc(tok.sem, 1)
                regs = None
                for it in self.q[e]:
                    if it[0] != "region":
                        run([it])
                        continue
                    if regs is None:
                        regs = [eng.value_load(self.ei[0:1, NX:NX + 1], min_val=0, max_val=NX)]
                        if e == "sp":
                            self.regs = {x: eng.value_load(self.ei[0:1, x:x + 1], min_val=0, max_val=NB - 1) for x in range(NX)}
                    kept = dict(seen)
                    with eng.If(regs[0] > it[2]):
                        run(it[1])
                    seen.clear()
                    seen.update(kept)
            deco(body)


class Bank:
    def __init__(self, t):
        self.t, self.free = t, []


def build(nc, A, out):
    from contextlib import ExitStack
    ctx = ExitStack()
    with ctx:
        P = Program(nc, ctx)
        op, dma = P.op, P.dma
        place = [(nc.sbuf_base + 63) // 64 * 64]
        names = [0]

        def sb(shape, dt=F32, name="t"):
            names[0] += 1
            size = int(np.prod(shape[1:])) * 4
            t = nc.alloc_sbuf_tensor_at(f"{name}_{names[0]}", shape, dt, offset=place[0])
            place[0] += (size + 63) // 64 * 64
            assert place[0] <= nc.sbuf_usable_end, (name, place[0], nc.sbuf_usable_end)
            return t

        def pair(shape, name="t"):
            return sb(shape, F32R, name + "H"), sb(shape, F32R, name + "L")

        def sem(name):
            names[0] += 1
            return ctx.enter_context(nc.semaphore(f"{name}{names[0]}"))

        banks = [Bank(ctx.enter_context(nc.psum_tensor(f"bank{i}", [128, 512], F32))) for i in range(8)]
        turn = [0]

        def bank():
            turn[0] = (turn[0] + 1) % 8
            return banks[turn[0]]

        sets = {"log_exp": "natural_log_exp_and_others", "silu": "silu_and_others", "sigmoid": "sigmoid_and_others",
                "trig": "trig_and_small"}

        def tables(name):
            if P.tables != name:
                P.tables = name
                op("act", lambda e: e.preload_act_table_set(sets[name]))

        x_place = place[0]
        xT = sb([128, 8, 512], F32, "xT")
        hH, hL = pair([128, 8, 512], "h")
        stage = [sb([128, CAP], F32, f"stage{i}") for i in range(NSTAGE)]
        wH = [sb([128, CAP], F32R, f"wH{i}") for i in range(NSPLIT)]
        wL = [sb([128, CAP], F32R, f"wL{i}") for i in range(NSPLIT)]
        cols = sb([128, NCOLS], F32, "cols")
        mats = sb([128, len(MATS), 128], F32, "mats")
        rmats = sb([128, len(RMATS), 128], F32R, "rmats")
        rident, rones = sb([128, 128], F32R, "rident"), sb([128, 128], F32R, "rones")
        rpos, rdm = rmats[:, 3, :], rmats[:, 4, :]
        mark0 = place[0]

        def col(name, k=0):
            at = COLS[name][0] + k
            return cols[:, at:at + 1]

        def mat(name):
            return mats[:, MATS.index(name), :]

        s_c = sem("s_c")
        t_x = []
        for k in range(4):
            s = sem("s_x")
            t_x += 2 * [dma("sp", lambda e, k=k, s=s: e.dma_start(xT[:, 2 * k:2 * k + 2, :], A["x"][:, 2 * k:2 * k + 2, :]).then_inc(s, 16), s)]
        dma("sp", lambda e: e.dma_start(cols[:, :], A["cols"]).then_inc(s_c, 16), s_c)
        nm = len(MATS) * 128
        t_c = dma("sp", lambda e: e.dma_start(mats[:, :, :].rearrange("p a b -> p (a b)"), A["mats"][:, 0:nm]).then_inc(s_c, 16), s_c)
        rstage = nc.alloc_sbuf_tensor_at("rstage", [128, len(RMATS) * 128], F32, offset=nc.sbuf_usable_end // 64 * 64 - 16384)

        t_const = []

        def operand_constants():
            s = sem("s_r")
            t = dma("sp", lambda e: e.dma_start(rstage[:, :], A["mats"][:, nm:]).then_inc(s, 16), s)
            op("act", lambda e: e.activation(rmats[:, :, :].rearrange("p a b -> p (a b)"), rstage[:, :], ACT.Copy), t)
            op("act", lambda e: e.activation(rident[:, :], mat("ident"), ACT.Copy), t_c)
            return op("act", lambda e: e.activation(rones[:, :], mat("ones"), ACT.Copy), t_c)

        xb_d = nc.dram_tensor("slot_rows", (NSLOT, 1024), F32).ap()
        yb_d = nc.dram_tensor("slot_results", (NSLOT, 1024), F32).ap()
        top_end = nc.sbuf_usable_end // 64 * 64 - 6144
        zero = nc.alloc_sbuf_tensor_at("zero", [128, 1024], F32, offset=top_end - 22528)
        s_z = sem("s_z")
        t_zero = [op("pool", lambda e: e.memset(zero[:, :], 0.0))]
        zeros = [d[n:min(n + 128, NSLOT), :] for d, a in ((xb_d, 0), (yb_d, NB * BLK)) for n in range(a, NSLOT, 128)]

        def store_zeros(n, *waits):
            for d in [zeros.pop() for _ in range(min(n, len(zeros)))]:
                t_zero.append(dma("pool", lambda e, d=d: e.dma_start(d, zero[0:d.shape[0], :]).then_inc(s_z, 16), s_z, t_zero[0], *waits))

        class Slot:
            def __init__(self, *t):
                self.t, self.sem, self.user, self.after = t, sem("s_stage"), None, []

        stream = {"stage": [Slot(t) for t in stage], "split": [Slot(a, b) for a, b in zip(wH, wL)], "ahead": AHEAD}
        units = []
        holes = []

        class Unit:
            pass

        def use(parts, k, n, ahead=True):
            i = len(units)
            u = Unit()
            size = k * n
            assert size <= CAP
            u.t_hi, u.t_lo, u.done = Tok("act"), Tok("dve"), None
            st_, sp_ = stream["stage"].pop(0), stream["split"].pop(0)
            stream["stage"].append(st_)
            stream["split"].append(sp_)
            s, slot = st_.sem, st_.t[0]
            dst_hi, dst_lo = sp_.t
            before = ([t for t in (st_.user.t_lo, st_.user.t_hi) if t] if st_.user else []) + st_.after
            reader = ([sp_.user.done] if sp_.user and sp_.user.done else []) + sp_.after
            st_.user = sp_.user = u
            st_.after, sp_.after = [], []

            def go(e):
                for at, src in parts:
                    src = src(e) if callable(src) else src
                    a, b = src.shape[-2], src.shape[-1]
                    e.dma_start(slot[:, at:at + a * b].rearrange("p (a b) -> p a b", a=a), src).then_inc(s, 16)
            u.landed = dma("sp", go, s, before, n=len(parts))
            while len(holes) <= (i + stream["ahead"] if ahead else i):
                holes.append((P.hold("act"), P.hold("dve")))
            for t in reader + [u.t_hi, u.t_lo]:
                t.used = True
            holes[i][0][:] = [lambda e: e.activation(dst_hi[:, 0:size], slot[:, 0:size], ACT.Copy), [u.landed] + reader, u.t_hi]
            holes[i][1][:] = [lambda e: e.tensor_tensor(dst_lo[:, 0:size], slot[:, 0:size], dst_hi[:, 0:size].bitcast(F32),
                                                        ALU.subtract), reader + [u.t_hi], u.t_lo]
            units.append(u)
            u.H = dst_hi[:, 0:size].rearrange("p (k n) -> p k n", k=k)
            u.L = dst_lo[:, 0:size].rearrange("p (k n) -> p k n", k=k)
            return u

        def hold_ahead():
            while len(holes) < len(units) + stream["ahead"]:
                holes.append((P.hold("act"), P.hold("dve")))

        def mm(outp, lhsT, rhs, start, stop, *waits, skip=False):
            return op("pe", lambda e: e.matmul(outp, lhsT, rhs, start=start, stop=stop, skip_group_check=skip), *waits)

        def mm3(outp, a, b, start, stop, *waits, skip=False):
            mm(outp, a[0], b[0], start, False, *waits, skip=skip)
            mm(outp, a[0], b[1], False, False, skip=skip)
            return mm(outp, a[1], b[0], False, stop, skip=skip)

        def split(src, H, L, *waits, scale=1.0):
            t1 = op("act", lambda e: e.activation(H, src, ACT.Copy, scale=scale), *waits)
            if scale == 1.0:
                return op("dve", lambda e: e.tensor_tensor(L, src, H.bitcast(F32), ALU.subtract), t1, *waits)
            return op("dve", lambda e: e.scalar_tensor_tensor(L, src, scale, H.bitcast(F32), ALU.mult, ALU.subtract), t1, *waits)

        def dense(parts, K, act, *waits, b=None, parts_ready=None):
            u = use(parts, K, 128)
            b = b or bank()
            w = [u.t_lo, u.t_hi, b.free, list(waits)]
            for k in range(K):
                last = mm3(b.t[:, :], (u.H[:, k, :], u.L[:, k, :]), (act[0][:, k, :], act[1][:, k, :]),
                           k == 0, k == K - 1, *(w if k == 0 else ()), *([parts_ready[k]] if parts_ready else ()))
            u.done = last
            return b, last

        def wcols(name, c0, n, k0=0, K=8):
            v = A[name].rearrange("(k p) n -> p k n", p=128)
            return v[:, k0:k0 + K, c0:c0 + n]

        tmp = {}

        class Ring:
            def __init__(self, n, shape, dt=F32, name="r"):
                self.t = [sb(shape, dt, name) for _ in range(n)]
                self.free = [[] for _ in range(n)]
                self.i = -1

            def get(self):
                self.i = (self.i + 1) % len(self.t)
                f = self.free[self.i]
                self.free[self.i] = []
                return self.t[self.i], f, self

            def release(self, *toks):
                self.free[self.i] = list(toks)

        def rings(ny=3, nsq=2):
            tmp["sq"] = Ring(nsq, [128, 512], name="sq")
            tmp["rr"] = Ring(2, [128, 512], name="rr")
            tmp["y"] = Ring(ny, [128, 512], name="y")

        acc = nc.alloc_sbuf_tensor_at("acc", [128, 512], F32, offset=top_end)
        xsq = [nc.alloc_sbuf_tensor_at(f"xsq{k}", [128, 512], F32, offset=top_end + 2048 + 2048 * k) for k in range(2)]
        summed = {"t": None, "n": 0, "free": [None, None]}

        def add_square(k, *waits):
            n = summed["n"] % 8
            summed["n"] += 1
            if n == 0:
                summed["t"] = op("act", lambda e: e.activation(acc[:, :], xT[:, k, :], ACT.Square), summed["t"], *waits)
                return
            q = xsq[n % 2]
            t = op("act", lambda e: e.activation(q[:, :], xT[:, k, :], ACT.Square), summed["free"][n % 2], *waits)
            summed["t"] = op("dve", lambda e: e.tensor_tensor(acc[:, :], acc[:, :], q[:, :], ALU.add), t, summed["t"])
            summed["free"][n % 2] = summed["t"]

        def norm_x(gain):
            b = bank()
            t = mm(b.t[:, :], mat("ones"), acc[:, :], True, True, summed["t"], b.free, t_c)
            r, f, _ = tmp["rr"].get()
            tables("log_exp")
            t1 = op("act", lambda e: e.activation(r[:, :], b.t[:, :], ACT.Ln, bias=col("eps"), scale=1.0 / 1024), t, f, t_c)
            b.free = [t1]
            summed["t"] = t1
            tables("log_exp")
            t2 = op("act", lambda e: e.activation(r[:, :], r[:, :], ACT.Exp, scale=-0.5), t1)
            tpe = P.last.get("pe")
            ts, last = [], None
            for k in range(8):
                y, f, _ = tmp["y"].get()
                slot = tmp["y"].i
                t3 = op("dve", lambda e, y=y, k=k: e.scalar_tensor_tensor(y[:, :], xT[:, k, :], col(gain, k), r[:, :], ALU.mult, ALU.mult), t2, f)
                t4 = op("act", lambda e, y=y, k=k: e.activation(hH[:, k, :], y[:, :], ACT.Copy), t3, tpe)
                if last:
                    ts.append(last())

                def last(y=y, k=k, t4=t4, slot=slot):
                    t5 = op("dve", lambda e: e.tensor_tensor(hL[:, k, :], y[:, :], hH[:, k, :].bitcast(F32), ALU.subtract), t4)
                    tmp["y"].free[slot] = [t5]
                    return t5
            ts.append(last())
            tmp["rr"].release(t3)
            return ts

        def rms(src, K, ones, D, *waits):
            sq, rr = tmp["sq"], tmp["rr"]
            b = bank()
            for k in range(K):
                s, f, _ = sq.get()
                t1 = op("act", lambda e, s=s, k=k: e.activation(s[:, :], src(k), ACT.Square), f, *waits)
                last = mm(b.t[:, :], ones, s[:, :], k == 0, k == K - 1, t1, b.free, t_c)
                sq.release(last)
            r, f, _ = rr.get()
            tables("log_exp")
            t1 = op("act", lambda e: e.activation(r[:, :], b.t[:, :], ACT.Ln, bias=col("eps"), scale=1.0 / D), last, f, t_c)
            b.free = [t1]
            tables("log_exp")
            return r, op("act", lambda e: e.activation(r[:, :], r[:, :], ACT.Exp, scale=-0.5), t1)

        def norm(src, K, ones, D, gain, out, *waits):
            r, t2 = rms(src, K, ones, D, *waits)
            for k in range(K):
                y, f, _ = tmp["y"].get()
                t3 = op("dve", lambda e, y=y, k=k: e.scalar_tensor_tensor(y[:, :], src(k), gain(k), r[:, :], ALU.mult, ALU.mult), t2, f, t_c, *waits)
                t4 = split(y[:, :], out[0][:, k, :], out[1][:, k, :], t3)
                tmp["y"].release(t4)
            tmp["rr"].release(t3)
            return t4

        def chunk_norm(b, t, ones, gain, out, scale=1.0, rope=None, before=()):
            y, f, _ = tmp["y"].get()
            ty = op("act", lambda e: e.activation(y[:, :], b.t[:, :], ACT.Copy), t, f)
            b.free = [ty]
            if gain is not None:
                r, t2 = rms(lambda k: y[:, :], 1, ones, 64, ty)
                ty = op("dve", lambda e: e.scalar_tensor_tensor(y[:, :], y[:, :], gain, r[:, :], ALU.mult, ALU.mult), t2, t_c)
                tmp["rr"].release(ty)
            if rope is not None:
                cs, sn, tr = rope
                b2 = bank()
                t2 = mm(b2.t[:, :], mat("perm"), y[:, :], True, True, ty, b2.free, t_c)
                z, f, _ = tmp["sq"].get()
                t3 = op("dve", lambda e: e.tensor_tensor(z[:, :], b2.t[:, :], sn[:, :], ALU.mult), t2, f, tr)
                b2.free = [t3]
                t4 = op("dve", lambda e: e.tensor_tensor(y[:, :], y[:, :], cs[:, :], ALU.mult), t2, ty, tr)
                ty = op("dve", lambda e: e.tensor_tensor(y[:, :], y[:, :], z[:, :], ALU.add), t3, t4)
                tmp["sq"].release(ty)
            t5 = split(y[:, :], out[0], out[1], ty, list(before), scale=scale)
            tmp["y"].release(t5)
            return t5

        def load(dst, src, *waits):
            s = sem("s_ld")
            return dma("pool", lambda e: e.dma_start(dst, src).then_inc(s, 16), s, *waits)

        FILL = (1, 1, (0, 1, 0, 1), (1, 1, 1, 1), 0, 3, 1, (3, 11, 27, 31))

        rope = []
        cs, sn = [nc.alloc_sbuf_tensor_at(n, [128, 512], F32, offset=top_end - 4096 + 2048 * k) for k, n in enumerate(("cs", "sn"))]

        def rope_tables():
            ang, nn = [nc.alloc_sbuf_tensor_at(n, [128, 512], F32, offset=top_end - 18432 + 2048 * k) for k, n in enumerate(("ang", "nn"))]
            posi = nc.alloc_sbuf_tensor_at("posi", [128, 512], I32, offset=top_end - 14336)
            tp = load(posi[:, :], A["positions"].partition_broadcast(128).rearrange("p a n -> p (a n)"))
            t = op("dve", lambda e: e.tensor_copy(ang[:, :], posi[:, :]), tp)
            t = op("dve", lambda e: e.tensor_scalar(ang[:, :], ang[:, :], col("inv_freq"), None, ALU.mult), t, t_c)
            magic = 12582912.0
            t = op("dve", lambda e: e.tensor_scalar(nn[:, :], ang[:, :], float(1 / (2 * np.pi)), magic, ALU.mult, ALU.add), t)
            t = op("dve", lambda e: e.tensor_scalar(nn[:, :], nn[:, :], magic, None, ALU.subtract), t)
            c1 = 6.28125
            c2 = float(np.float32(np.round((2 * np.pi - c1) * 2 ** 21) / 2 ** 21))
            c3 = float(2 * np.pi - c1 - c2)
            for c in (c1, c2, c3):
                t = op("dve", lambda e, c=c: e.scalar_tensor_tensor(ang[:, :], nn[:, :], -c, ang[:, :], ALU.mult, ALU.add), t)
            t = op("dve", lambda e: e.tensor_scalar(ang[:, :], ang[:, :], 3.1415925, -3.1415925, ALU.min, ALU.max), t)
            tables("silu")
            t1 = op("act", lambda e: e.activation(sn[:, :], ang[:, :], ACT.Sin), t)
            tables("silu")
            t2 = op("act", lambda e: e.activation(cs[:, :], ang[:, :], ACT.Sin, scale=0.5), t)
            t = op("dve", lambda e: e.tensor_tensor(cs[:, :], cs[:, :], cs[:, :], ALU.mult), t2)
            t = op("dve", lambda e: e.tensor_scalar(cs[:, :], cs[:, :], -2.0, 1.0, ALU.mult, ALU.add), t)
            t = op("dve", lambda e: e.tensor_scalar(sn[:, :], sn[:, :], col("sgn"), None, ALU.mult), t1, t)
            rope.extend((cs, sn, t))

        def ffn(gate, up, down, gain):
            place[0] = mark0
            rings()
            hid = pair([128, 11, 512], "hid")
            sg = Ring(2, [128, 512], name="sg")
            hf = Ring(3, [128, 512], name="hf")
            ths = norm_x(gain)
            if gain == "g_ffn1":
                t_const.append(operand_constants())
            t_down = None
            for half in range(2):
                for m in range(11):
                    c0 = (half * 11 + m) * 128
                    bg, tg = dense([(0, wcols(gate, c0, 128))], 8, h, parts_ready=ths if m == 0 and half == 0 else None)
                    bu, tu = dense([(0, wcols(up, c0, 128))], 8, h)
                    s, f, _ = sg.get()
                    tables("silu")
                    t1 = op("act", lambda e, s=s, b=bg: e.activation(s[:, :], b.t[:, :], ACT.Silu), tg, f)
                    bg.free = [t1]
                    y, f, _ = hf.get()
                    t2 = op("dve", lambda e, y=y, s=s, b=bu: e.tensor_tensor(y[:, :], s[:, :], b.t[:, :], ALU.mult), t1, tu, f)
                    bu.free = [t2]
                    sg.release(t2)
                    t3 = split(y[:, :], hid[0][:, m, :], hid[1][:, m, :], t2, t_down)
                    hf.release(t3)
                    store_zeros(3, t3)
                    if gain == "g_ffn1" and half == 1 and m == 2:
                        rope_tables()
                for m in range(8):
                    b, t_down = dense([(0, wcols(down, m * 128, 128, half * 11, 11))], 11, hid, t3)
                    tx = op("dve", lambda e, b=b, m=m: e.scalar_tensor_tensor(xT[:, m, :], b.t[:, :], 0.5, xT[:, m, :], ALU.mult, ALU.add), t_down)
                    b.free = [tx]
                    if half == 1:
                        add_square(m, tx)
            P.barrier(also=t_zero[-1:])
            return tx

        REG = [(0, 0, 0), (1, 0, 512), (2, 0, 1024), (1, 384, 896)]

        def token_rows(unit_parts, n, dst_banks, act, *waits):
            for kk in range(4):
                u = use([(0, unit_parts(kk))], 2, n)
                for tt in range(4):
                    for j in range(2):
                        k = 2 * kk + j
                        last = mm3(dst_banks[tt].t[:, 0:n], (act[0][:, k, tt * 128:(tt + 1) * 128], act[1][:, k, tt * 128:(tt + 1) * 128]),
                                   (u.H[:, j, :], u.L[:, j, :]), k == 0, k == 7,
                                   *([u.t_lo, u.t_hi, dst_banks[tt].free, list(waits)] if j == 0 else []))
                u.done = last
            return last

        def mixer1():
            place[0] = mark0
            cq = pair([128, 2, 512], "cq")
            cqf = sb([128, 2, 512], F32, "cqf")
            rl = Ring(2, [128, 512], name="rl")
            assert place[0] <= mark0 + (1 << 14)
            place[0] = mark0
            ya = pair([128, 4, 512], "ya")
            mark1 = place[0]
            qa = pair([128, 4, 512], "qa")
            ka = pair([128, 512], "ka")
            va = pair([128, 4, 128], "va")
            amask = sb([128, 1280], F32R, "amask")
            widx = sb([128, 4, 8], F32, "widx")
            wuv = pair([128, 4, 128], "wuv")
            mark2 = place[0]
            rings()
            qi = pair([128, 4, 512], "qi")
            ki = pair([128, 512], "ki")
            at = place[0]
            wuvF = sb([128, 8, 64], F32, "wuvF")
            place[0] = at

            ths = norm_x("g_mix")
            tw = load(wuvF[:, :, :], A["w_uv_a"].rearrange("h c d -> c h d"), P.last["act"], P.last["dve"], P.last["pe"])
            gate_d = nc.dram_tensor("gates", (16, 128, 512), F32).ap()
            gt = [nc.alloc_sbuf_tensor_at(f"gt{k}", [128, 512], F32, offset=top_end + 2048 + 2048 * k) for k in range(2)]
            gate_free, gate_t = list(summed["free"]), []
            s_gate = [sem("s_gate") for _ in range(2)]

            def fill(count, b=None):
                for _ in range(count):
                    n = len(gate_t)
                    if n == 16:
                        return
                    b, t = dense([(0, wcols("w_in", 2056 + 1024 * (n % 2) + (n // 2) * 128, 128))], 8, h, b=b)
                    g, k = gt[n % 2], n % 2
                    t = op("act", lambda e, b=b, g=g: e.activation(g[:, :], b.t[:, :], ACT.Copy), t, gate_free if gt[0] is gt[1] else gate_free[k])
                    b.free = [t]
                    gate_t.append(dma("pool", lambda e, n=n, g=g, k=k: e.dma_start(gate_d[n], g[:, :]).then_inc(s_gate[k], 16), s_gate[k], t))
                    gate_free[k] = gate_t[-1]

            for m in range(2):
                b, t = dense([(0, wcols("w_in", m * 128, 128))], 8, h, parts_ready=ths if m == 0 else None)
                tq = op("act", lambda e, b=b, m=m: e.activation(cqf[:, m, :], b.t[:, :], ACT.Copy), t)
                b.free = [tq]
            bk, tk = dense([(0, wcols("w_k2", 128, 128))], 8, h)
            fill(FILL[0])
            tki = chunk_norm(bk, tk, None, None, (ki[0][:, :], ki[1][:, :]), rope=rope)
            tcq = norm(lambda k: cqf[:, k, :], 2, mat("ones"), 256, lambda k: col("g_cq", k), cq, tq)
            vb4 = [banks[i] for i in range(4)]
            tv = token_rows(lambda kk: wcols("w_vw", 0, 136, 2 * kk, 2), 136, vb4, h)
            for tt in range(4):
                t1 = split(vb4[tt].t[:, 0:128], va[0][:, tt, :], va[1][:, tt, :], tv)
                t2 = op("dve", lambda e, tt=tt: e.tensor_scalar(widx[:, tt, :], vb4[tt].t[:, 128:136], float((8 ** -0.5) * (64 ** -0.5)), None, ALU.mult), t1)
                vb4[tt].free = [t2]
            tva = t2
            for m in range(4):
                b, t = dense([(0, wcols("w_q_idx", m * 128, 128, 0, 2))], 2, cq, tcq)
                fill(FILL[2][m])
                tqi = chunk_norm(b, t, None, None, (qi[0][:, m, :], qi[1][:, m, :]), rope=rope)
            split(wuvF[:, :, :].rearrange("p (a b) d -> p a (b d)", b=2), wuv[0][:, :, :], wuv[1][:, :, :], tw)
            W0 = [0, 128, 384, 768]
            sc = [None, nc.alloc_sbuf_tensor_at("score1", [128, 256], F32, offset=top_end)] + [sb([128, 128 * (i + 1)], F32, "score") for i in range(2, 4)]
            top = nc.alloc_sbuf_tensor_at("top", [128, 8], F32, offset=top_end + 1024)
            assert place[0] <= top_end - 4096
            t = op("act", lambda e: e.activation(amask[:, 0:128], mat("tru"), ACT.Copy, scale=NEG), t_c, P.last["dve"])
            tm = [t, None, None, None]
            rounds = [(i, rnd) for i in range(1, 4) for rnd in range(16)]

            def topk(count):
                for i, rnd in [rounds.pop(0) for _ in range(min(count, len(rounds)))]:
                    t = op("dve", lambda e, i=i: e.max(top[:, :], sc[i][:, :]), tm[i])
                    tm[i] = op("dve", lambda e, i=i: e.match_replace(sc[i][:, :], top[:, :], sc[i][:, :], REPL), t)
                    if rnd == 15:
                        W = 128 * (i + 1)
                        tm[i] = op("dve", lambda e, i=i, W=W: e.tensor_scalar(amask[:, W0[i]:W0[i] + W], sc[i][:, :], -2.0e38, NEG, ALU.is_gt, ALU.mult), tm[i])

            for i in range(1, 4):
                W = 128 * (i + 1)
                for hd in range(8):
                    if i > 1:
                        topk(FILL[6])
                    c, po = hd // 2, 64 * (hd % 2)
                    b = bank()
                    t1 = mm3(b.t[:, 0:W], [x[po:po + 64, c, i * 128:(i + 1) * 128] for x in qi],
                             [x[po:po + 64, 0:W] for x in ki], True, True, tqi, tki, b.free)
                    r, f, _ = rl.get()
                    t2 = op("act", lambda e, r=r, b=b, W=W: e.activation(r[:, 0:W], b.t[:, 0:W], ACT.Relu), t1, f)
                    b.free = [t2]
                    if hd == 0:
                        t3 = op("dve", lambda e, r=r, i=i, W=W, hd=hd: e.tensor_scalar(sc[i][:, :], r[:, 0:W], widx[:, i, hd:hd + 1], None, ALU.mult), t2, tva)
                    else:
                        t3 = op("dve", lambda e, r=r, i=i, W=W, hd=hd: e.scalar_tensor_tensor(sc[i][:, :], r[:, 0:W], widx[:, i, hd:hd + 1], sc[i][:, :], ALU.mult, ALU.add), t2, t3)
                    rl.release(t3)
                t3 = op("dve", lambda e, i=i: e.scalar_tensor_tensor(sc[i][:, i * 128:], mat("tru"), NEG, sc[i][:, i * 128:], ALU.mult, ALU.add), t3)
                tm[i] = t3
                fill(FILL[4])
            bt, tt_ = dense([(0, wcols("w_k2", 0, 128))], 8, h)
            topk(4)
            fill(FILL[1])
            topk(3)
            tka = chunk_norm(bt, tt_, mat("blk64"), col("g_k_a"), (ka[0][:, :], ka[1][:, :]), rope=rope)
            for m in range(4):
                b, t = dense([(0, wcols("w_uq_a", m * 128, 128, 0, 2))], 2, cq)
                topk(FILL[5])
                fill(FILL[3][m])
                topk(3)
                tqa = chunk_norm(b, t, mat("blk64"), col("g_q_a"), (qa[0][:, m, :], qa[1][:, m, :]), scale=0.125, rope=rope)
            topk(48)
            P.barrier()

            place[0] = mark2
            PT = [pair([128, 4, 4, 128], "PT") for _ in range(2)]
            ptfree = [[], []]
            pr = Ring(3, [128, 512], name="p")
            ol = [pair([128, 512], "ol")] * 2
            olfree = [[], []]
            st = sb([128, 64, 2], F32, "st")
            jobs = [(i, g, hh) for i in range(4) for g in range(2) for hh in range(4)]
            ready = {}

            def softmax_rows(b, t, W, p, f, n):
                t1 = op("dve", lambda e: e.tensor_reduce(st[:, n, 0:1], b.t[:, 0:W], AX.X, ALU.max), t)
                t1 = op("dve", lambda e: e.tensor_scalar(st[:, n, 0:1], st[:, n, 0:1], -1.0, None, ALU.mult), t1)
                tables("log_exp")
                t2 = op("act", lambda e: e.activation(p[:, 0:W], b.t[:, 0:W], ACT.Exp, bias=st[:, n, 0:1], accum_out=st[:, n, 1:2]), t1, f)
                b.free = [t2]
                return op("dve", lambda e: e.reciprocal(st[:, n, 1:2], st[:, n, 1:2]), t2)

            def first(n):
                i, g, hh = jobs[n]
                hd = 4 * g + hh
                c, po, W = hd // 2, 64 * (hd % 2), 128 * (i + 1)
                b = bank()
                mm(b.t[:, 0:W], rident[:, :], amask[:, W0[i]:W0[i] + W], True, False, b.free, tm[i], t_const[0])
                t = mm3(b.t[:, 0:W], [x[po:po + 64, c, i * 128:(i + 1) * 128] for x in qa],
                        [x[po:po + 64, 0:W] for x in ka], False, True)
                p, f, _ = pr.get()
                t2 = softmax_rows(b, t, W, p, f, n)
                t3 = op("dve", lambda e: e.tensor_scalar(p[:, 0:W], p[:, 0:W], st[:, n, 1:2], None, ALU.mult), t2)
                ready[n] = (p, t3)

            def second(n):
                i, g, hh = jobs[n]
                p, t = ready.pop(n)
                b = bank()
                for s in range(i + 1):
                    t1 = op("pe", lambda e, s=s, b=b: e.transpose(b.t[:, s * 128:(s + 1) * 128], p[:, s * 128:(s + 1) * 128], mat("ident")), t, b.free)
                pr.free[n % 3] = [t1]
                k = (n // 4) % 2
                src = b.t[:, 0:128 * (i + 1)].rearrange("p (s n) -> p s n", n=128)
                t2 = split(src, PT[k][0][:, 0:i + 1, hh, :], PT[k][1][:, 0:i + 1, hh, :], t1, ptfree[k])
                b.free = [t2]
                if hh < 3:
                    return

                def values():
                    b = bank()
                    for s in range(i + 1):
                        t3 = mm3(b.t[:, :], (va[0][:, s, :], va[1][:, s, :]),
                                 [x[:, s, :, :] for x in PT[k]], s == 0, s == i, t2, b.free)
                    ptfree[k] = [t3]
                    t4 = split(b.t[:, :], ol[k][0][:, :], ol[k][1][:, :], t3, olfree[0])
                    b.free = [t4]
                    later.append(lambda: expand(t4))

                def expand(t4):
                    for c2 in range(2):
                        c = 2 * g + c2
                        b = bank()
                        t5 = mm3(b.t[:, 0:256], (wuv[0][:, c, :], wuv[1][:, c, :]), [x[:, 256 * c2:256 * c2 + 256] for x in ol[k]], True, True, t4, b.free)
                        for e2 in range(2):
                            pp = slice(64 * e2, 64 * e2 + 64)
                            t6 = split(b.t[pp, 128 * e2:128 * e2 + 128], ya[0][pp, c, i * 128:(i + 1) * 128], ya[1][pp, c, i * 128:(i + 1) * 128], t5)
                        b.free = [t6]
                        olfree[0] = [t5]
                    y_done.append(t6)
                later.append(values)

            later, y_done = [], []

            def run_later():
                now = later[:]
                del later[:]
                for f in now:
                    f()

            for n in range(len(jobs) + 2):
                if n < len(jobs):
                    first(n)
                run_later()
                if n >= 2:
                    second(n - 2)
                if n in FILL[7]:
                    fill(1)
            run_later()
            run_later()
            tya = y_done[-1]
            P.barrier(also=gate_free)

            place[0] = mark1
            yb = pair([128, 4, 512], "yb")
            vb = pair([128, 4, 512], "vb")
            qb = [pair([128, 512], "qb") for _ in range(2)]
            kb = [pair([128, 512], "kb") for _ in range(2)]
            T = [sb([128, 1280], F32, "T") for _ in range(2)]
            SP = [pair([128, 1280], "SP") for _ in range(2)]
            gt[:] = [sb([128, 512], F32, "gt")] * 2
            vbanks = banks[0:4]
            t = token_rows(lambda kk: wcols("w_in", 1544, 512, 2 * kk, 2), 512, vbanks, h)
            for tt in range(4):
                tvb = split(vbanks[tt].t[:, :], vb[0][:, tt, :], vb[1][:, tt, :], t)
                vbanks[tt].free = [tvb]
            zb = [banks[0:3], banks[3:6]]
            pvb = banks[6:8]
            z_t, s_t, a_t, qk_t = {}, {}, {}, {}
            qkfree = [[], []]
            spfree = [[], []]

            def project(c, which):
                dst = (qb, kb)[which][c % 2]
                b, t = dense([(0, wcols("w_in", (520, 1032)[which] + c * 128, 128))], 8, h, b=pvb[1 - which])
                t = split(b.t[:, :], dst[0][:, :], dst[1][:, :], t, qkfree[c % 2], scale=(0.125, 1.0)[which])
                b.free = [t]
                qk_t.setdefault(c, []).append(t)

            def b1(hd):
                c, po, z = hd // 2, slice(64 * (hd % 2), 64 * (hd % 2) + 64), zb[hd % 2]
                for j in range(4):
                    bk_, off, _ = REG[j]
                    N = 512 - 128 * j
                    o = z[bk_].t[:, off:off + N]
                    mm3(o, [x[po, 128 * j:128 * j + 128] for x in kb[c % 2]], [x[po, 128 * j:512] for x in qb[c % 2]],
                        j != 3, False, qk_t[c], z[bk_].free, skip=True)
                    t = mm(z[bk_].t[:, off:off + 128], rident[:, :], rmats[:, 2, :], False, True, t_const[0], skip=True)
                qkfree[c % 2] = [t]
                x = T[hd % 2]
                for bk_, o, n in ((0, 0, 512), (1, 512, 512), (2, 1024, 256)):
                    t1 = op("act", lambda e, bk_=bk_, o=o, n=n: e.activation(x[:, o:o + n], z[bk_].t[:, 0:n], ACT.Abs), t, spfree[hd % 2])
                tables("log_exp")
                t1 = op("act", lambda e: e.activation(x[:, :], x[:, :], ACT.Exp, scale=-1.0), t1)
                tables("log_exp")
                t1 = op("act", lambda e: e.activation(x[:, :], x[:, :], ACT.Ln, bias=col("one")), t1, t_c)
                for bk_, o, n in ((0, 0, 512), (1, 512, 512), (2, 1024, 256)):
                    t2 = op("dve", lambda e, bk_=bk_, o=o, n=n: e.scalar_tensor_tensor(x[:, o:o + n], z[bk_].t[:, 0:n], 0.0, x[:, o:o + n], ALU.max, ALU.add), t1)
                s_t[hd] = split(x[:, :], SP[hd % 2][0][:, :], SP[hd % 2][1][:, :], t2, spfree[hd % 2])

            def b2(hd):
                z, sp, x = zb[hd % 2], SP[hd % 2], T[hd % 2]
                for j in range(4):
                    bk_, off, o = REG[j]
                    for j2 in range(j, 4):
                        o2, N = REG[j2][2], 512 - 128 * j2
                        w = rmats[:, 0, :] if j2 == j else rmats[:, 1, :]
                        d = z[bk_].t[:, off + 128 * (j2 - j):off + 128 * (j2 - j) + N]
                        for part in sp:
                            t = mm(d, w, part[:, o2:o2 + N], False, True, s_t[hd], skip=True)
                for bk_, o, n in ((0, 0, 512), (1, 512, 512), (2, 1024, 256)):
                    tables("log_exp")
                    t1 = op("act", lambda e, bk_=bk_, o=o, n=n: e.activation(x[:, o:o + n], z[bk_].t[:, 0:n], ACT.Exp), t, s_t[hd])
                for bb in z:
                    bb.free = [t1]
                a_t[hd] = split(x[:, :], sp[0][:, :], sp[1][:, :], t1, t)

            def b3(hd):
                c, pp = hd // 2, slice(64 * (hd % 2), 64 * (hd % 2) + 64)
                b, a = pvb[hd % 2], SP[hd % 2]
                for j in range(4):
                    o, N = REG[j][2], 512 - 128 * j
                    t = mm3(b.t[:, 128 * j:512], (vb[0][:, j, c * 128:(c + 1) * 128], vb[1][:, j, c * 128:(c + 1) * 128]),
                            [v[:, o:o + N] for v in a], j == 0, j == 3, a_t[hd], tvb, b.free)
                spfree[hd % 2] = [t]
                t1 = split(b.t[pp, :], yb[0][pp, c, :], yb[1][pp, c, :], t)
                b.free = [t1]
                return t1

            project(0, 0)
            project(0, 1)
            for hd in range(10):
                if hd < 6:
                    project(hd // 2 + 1, hd % 2)
                elif len(gate_t) < 16:
                    fill(1, pvb[1 - hd % 2])
                if hd >= 2:
                    tyb = b3(hd - 2)
                if 1 <= hd <= 8:
                    b2(hd - 1)
                if hd < 8:
                    b1(hd)
            fill(16)
            P.barrier(also=gate_free)

            place[0] = mark1 + (1 << 14)
            mg = pair([128, 8, 512], "mg")
            sg = Ring(4, [128, 512], name="sg")
            mt = Ring(2, [128, 512], name="mt")
            s_sg = [sem("s_sg") for _ in range(4)]
            loaded = {}

            def load_gate(n):
                g, f, _ = sg.get()
                k = sg.i
                loaded[n] = (g, k, dma("pool", lambda e, g=g, n=n, k=k: e.dma_start(g[:, :], gate_d[n]).then_inc(s_sg[k], 16), s_sg[k], f, gate_t[n], P.last["act"]))
            for n in range(4):
                load_gate(n)
            for m in range(8):
                u = use([(0, wcols("w_o_a", m * 128, 128, 0, 4)), (512, wcols("w_o_b", m * 128, 128, 0, 4))], 8, 128)
                ba, bb = bank(), bank()
                for k in range(4):
                    ta = mm3(ba.t[:, :], (u.H[:, k, :], u.L[:, k, :]), (ya[0][:, k, :], ya[1][:, k, :]), k == 0, k == 3, u.t_lo, u.t_hi, ba.free)
                for k in range(4):
                    tb = mm3(bb.t[:, :], (u.H[:, 4 + k, :], u.L[:, 4 + k, :]), (yb[0][:, k, :], yb[1][:, k, :]), k == 0, k == 3, bb.free)
                u.done = tb
                (s1, k1, l1), (s2, k2, l2) = loaded[2 * m], loaded[2 * m + 1]
                tables("sigmoid")
                t1 = op("act", lambda e, s=s1: e.activation(s[:, :], s[:, :], ACT.Sigmoid), l1)
                y, f, _ = mt.get()
                t2 = op("dve", lambda e, s=s1, b=ba, y=y: e.tensor_tensor(y[:, :], s[:, :], b.t[:, :], ALU.mult), t1, ta, f)
                ba.free = [t2]
                sg.free[k1] = [t2]
                tables("sigmoid")
                t3 = op("act", lambda e, s=s2: e.activation(s[:, :], s[:, :], ACT.Sigmoid), l2)
                t4 = op("dve", lambda e, s=s2, b=bb: e.tensor_tensor(s[:, :], s[:, :], b.t[:, :], ALU.mult), t3, tb)
                bb.free = [t4]
                t5 = op("dve", lambda e, s=s2, y=y: e.tensor_tensor(y[:, :], y[:, :], s[:, :], ALU.add), t4, t2)
                sg.free[k2] = [t5]
                if m < 6:
                    load_gate(2 * m + 4)
                    load_gate(2 * m + 5)
                tmg = split(y[:, :], mg[0][:, m, :], mg[1][:, m, :], t5)
                mt.release(tmg)
            for m in range(8):
                b, t = dense([(0, wcols("w_out", m * 128, 128))], 8, mg, tmg)
                tx = op("dve", lambda e, b=b, m=m: e.tensor_tensor(xT[:, m, :], b.t[:, :], xT[:, m, :], ALU.add), t)
                b.free = [tx]
                add_square(m, tx)
            P.barrier()
            return tx

        OUT = (7, 11, 12, 13, 14, 15, 16, 17)

        def mixer2():
            place[0] = mark0
            hm = pair([128, 4, 512], "hm")
            at = place[0]
            D = sb([128, 1280], F32, "D")
            S = pair([128, 1280], "S")
            place[0] = at
            ha = pair([128, 4, 512], "ha")
            mark1 = place[0]
            rings(2, 1)
            mv = pair([128, 4, 512], "mv")
            mark2 = place[0]
            ths = norm_x("norm1")

            rows = [sb([4, 512], F32, "row") for _ in range(4)]
            ir, fr, br, mr = rows
            gcol = sb([128, 4, 4], F32, "gcol")
            lam = sb([128, 4], F32, "lam")
            t_on = op("dve", lambda e: e.memset(mr[:, :], 1.0), P.last["dve"])
            b, t = dense([(0, wcols("w_if", 0, 128))], 8, h, parts_ready=ths)
            t1 = op("dve", lambda e, b=b: e.tensor_scalar(ir[:, :], b.t[0:4, :], col("bi")[0:4, :], None, ALU.add), t, t_c)
            t2 = op("dve", lambda e, b=b: e.tensor_copy(fr[:, :], b.t[32:36, :]), t)
            b.free = [t2]
            t2 = op("dve", lambda e: e.tensor_scalar(fr[:, :], fr[:, :], col("bf")[0:4, :], None, ALU.add), t2)
            t3 = op("act", lambda e: e.activation(br[:, :], fr[:, :], ACT.Abs), t2)
            tables("log_exp")
            t3 = op("act", lambda e: e.activation(br[:, :], br[:, :], ACT.Exp, scale=-1.0), t3)
            tables("log_exp")
            t3 = op("act", lambda e: e.activation(br[:, :], br[:, :], ACT.Ln, bias=col("one")[0:4, :]), t3)
            t3 = op("dve", lambda e: e.scalar_tensor_tensor(fr[:, :], fr[:, :], 0.0, br[:, :], ALU.min, ALU.subtract), t3)
            t3 = op("dve", lambda e: e.tensor_tensor_scan(br[:, :], mr[:, :], fr[:, :], 0.0, ALU.mult, ALU.add), t3, t_on)
            tg = op("dve", lambda e: e.tensor_tensor(ir[:, :], ir[:, :], br[:, :], ALU.subtract), t3, t1)
            tG = op("dve", lambda e: e.tensor_tensor_scan(fr[:, :], ir[:, :], ir[:, :], 0.0, ALU.max, ALU.max), tg)
            tM = op("dve", lambda e: e.tensor_tensor(mr[:, :], br[:, :], fr[:, :], ALU.add), tG)
            b = bank()
            for s in range(4):
                t = op("pe", lambda e, s=s, b=b: e.transpose(b.t[:, 4 * s:4 * s + 4], ir[:, 128 * s:128 * s + 128], mat("ident")[0:4, 0:4]), tg, b.free)
            tgc = op("dve", lambda e, b=b: e.tensor_copy(gcol[:, :, :].rearrange("p a b -> p (a b)"), b.t[:, 0:16]), t)
            b.free = [tgc]

            vbanks = banks[0:4]
            t = token_rows(lambda kk: wcols("w_in_2", 1024, 512, 2 * kk, 2), 512, vbanks, h)
            for tt in range(4):
                tmv = split(vbanks[tt].t[:, :], mv[0][:, tt, :], mv[1][:, tt, :], t)
                vbanks[tt].free = [tmv]

            raw = [sb([128, 515], F32, "raw")]
            cv = Ring(2, [128, 512], name="cv")
            mq, mk = [pair([128, 512], "mq") for _ in range(2)], [pair([128, 512], "mk") for _ in range(2)]
            so = [sb([128, 512], F32, "so")] * 2
            em = sb([128, 512], F32, "em")
            tz = [op("dve", lambda e, x=x: e.memset(x[:, 0:3], 0.0), P.last["dve"]) for x in raw]
            qk_t, so_t, rawfree, qkfree, sofree = {}, {}, [[], []], [[], []], [[], []]

            def conv_chunk(m, out, waits, scale):
                x = raw[0]
                b, t = dense([(0, wcols("w_in_2", m * 128, 128))], 8, h)
                t1 = op("act", lambda e: e.activation(x[:, 3:515], b.t[:, :], ACT.Copy), t, tz, rawfree[0])
                b.free = [t1]
                y, f, _ = cv.get()
                t2 = op("dve", lambda e: e.tensor_scalar(y[:, :], x[:, 0:512], col("conv_w", m), col("conv_b", m), ALU.mult, ALU.add), t1, tz, f, t_c)
                for j in range(1, 4):
                    t2 = op("dve", lambda e, j=j: e.scalar_tensor_tensor(y[:, :], x[:, j:j + 512], col("conv_w", 8 * j + m), y[:, :], ALU.mult, ALU.add), t2)
                rawfree[0] = [t2]
                tables("silu")
                t3 = op("act", lambda e: e.activation(y[:, :], y[:, :], ACT.Silu), t2)
                t4 = split(y[:, :], out[0][:, :], out[1][:, :], t3, waits, scale=scale)
                cv.release(t4)
                return t4

            def prepare(hd):
                k = hd % 2
                t1 = conv_chunk(hd, mq[k], qkfree[k], 1.0)
                t2 = conv_chunk(4 + hd, mk[k], qkfree[k], float(128 ** -0.5))
                qk_t[hd] = [t1, t2]

            dfree, sfree, emfree = [], [], []
            s_t, em_t, y_t = {}, {}, {}

            def head_a(hd):
                nonlocal dfree
                k = hd % 2
                b, t = dense([(0, wcols("w_in_2", 1536 + hd * 128, 128))], 8, h)
                tables("sigmoid")
                so_t[hd] = op("act", lambda e: e.activation(so[k][:, :], b.t[:, :], ACT.Sigmoid), t, sofree[0])
                b.free = [so_t[hd]]
                bG, bD, bM = bank(), bank(), bank()
                sel = mat("ident")[0:4, hd:hd + 1].broadcast_to([4, 128])
                tgb = mm(bG.t[:, :], sel, fr[:, :], True, True, tG, bG.free)
                mm(bD.t[:, :], sel, fr[:, :], True, False, bD.free, skip=True)
                for j in range(4):
                    tdb = mm(bD.t[:, 128 * j:128 * j + 128], rident[:, :], rpos[:, :], False, j == 3, t_const[0], skip=True)
                tmb = mm(bM.t[:, :], sel, mr[:, :], True, True, tM, bM.free)
                tables("log_exp")
                t1 = op("act", lambda e: e.activation(em[:, :], bM.t[:, :], ACT.Exp, scale=-1.0), tmb, emfree)
                bM.free = [t1]
                for j in range(4):
                    o, N = REG[j][2], 512 - 128 * j
                    tables("log_exp")
                    t2 = op("act", lambda e, o=o, j=j: e.activation(D[:, o:o + 128], bD.t[:, 128 * j:128 * j + 128], ACT.Exp, bias=gcol[:, j, hd:hd + 1], scale=-1.0), tdb, tgc, dfree)
                bD.free = [t2]
                for j in range(3):
                    o, N = REG[j][2], 512 - 128 * j
                    tables("log_exp")
                    t2 = op("act", lambda e, o=o, j=j, N=N: e.activation(D[:, o + 128:o + N], bG.t[:, 128 * j + 128:512], ACT.Exp, bias=gcol[:, j, hd:hd + 1], scale=-1.0), tgb)
                bG.free = [t2]
                zs = [bank(), bank(), bank()]
                for j in range(4):
                    bk_, off, o = REG[j]
                    N = 512 - 128 * j
                    t3 = mm3(zs[bk_].t[:, off:off + N], [x[:, 128 * j:128 * j + 128] for x in mk[k]], [x[:, 128 * j:512] for x in mq[k]],
                             True, True, qk_t[hd], zs[bk_].free, skip=True)
                qkfree[k] = [t3]
                for bk_, o, n in ((0, 0, 512), (1, 512, 512), (2, 1024, 256)):
                    t4 = op("dve", lambda e, bk_=bk_, o=o, n=n: e.tensor_tensor(D[:, o:o + n], zs[bk_].t[:, 0:n], D[:, o:o + n], ALU.mult), t3, t2)
                for bb in zs:
                    bb.free = [t4]
                t5 = split(D[:, :], S[0][:, :], S[1][:, :], t4, sfree)
                dfree = [t5]
                s_t[hd], em_t[hd] = t5, t1

            def head_b(hd):
                nonlocal sfree, emfree
                k, t5, t1 = hd % 2, s_t[hd], em_t[hd]
                bn, bd = bank(), bank()
                for j in range(4):
                    o, N = REG[j][2], 512 - 128 * j
                    t6 = mm3(bn.t[:, 128 * j:512], (mv[0][:, j, hd * 128:hd * 128 + 128], mv[1][:, j, hd * 128:hd * 128 + 128]),
                             [x[:, o:o + N] for x in S], j == 0, j == 3, t5, tmv, bn.free)
                for j in range(4):
                    o, N = REG[j][2], 512 - 128 * j
                    for part in S:
                        t7 = mm(bd.t[:, 128 * j:512], rones[:, :], part[:, o:o + N], j == 0 and part is S[0], j == 3 and part is S[1], t_const[0], bd.free)
                sfree = [t7]
                a, f, _ = tmp["sq"].get()
                ta = op("act", lambda e: e.activation(a[:, :], bd.t[:, :], ACT.Abs), t7, f)
                bd.free = [ta]
                ta = op("dve", lambda e: e.tensor_tensor(a[:, :], a[:, :], em[:, :], ALU.max), ta, t1)
                emfree = [ta]
                tables("log_exp")
                ta = op("act", lambda e: e.activation(a[:, :], a[:, :], ACT.Ln), ta)
                tables("log_exp")
                ta = op("act", lambda e: e.activation(a[:, :], a[:, :], ACT.Exp, scale=-1.0), ta)
                y, f, _ = tmp["y"].get()
                ty = op("dve", lambda e: e.tensor_tensor(y[:, :], bn.t[:, :], a[:, :], ALU.mult), ta, t6, f)
                bn.free = [ty]
                tmp["sq"].release(ty)
                ty = op("dve", lambda e: e.tensor_tensor(y[:, :], y[:, :], so[k][:, :], ALU.mult), ty, so_t[hd])
                sofree[0] = [ty]
                y_t[hd] = (y, tmp["y"].i, ty)

            def head_c(hd):
                y, slot, ty = y_t[hd]
                r, tr = rms(lambda q: y[:, :], 1, mat("ones"), 128, ty)
                ty = op("dve", lambda e: e.scalar_tensor_tensor(y[:, :], y[:, :], col("m_norm"), r[:, :], ALU.mult, ALU.mult), tr)
                tmp["rr"].release(ty)
                t8 = split(y[:, :], hm[0][:, hd, :], hm[1][:, hd, :], ty)
                tmp["y"].free[slot] = [t8]
                return t8

            prepare(0)
            head_a(0)
            for hd in range(4):
                if hd < 3:
                    prepare(hd + 1)
                head_b(hd)
                if hd < 3:
                    head_a(hd + 1)
                    head_c(hd)
            av = mv
            t = token_rows(lambda kk: wcols("w_in_2", 3080, 512, 2 * kk, 2), 512, vbanks, h)
            for tt in range(4):
                tav = split(vbanks[tt].t[:, :], av[0][:, tt, :], av[1][:, tt, :], t)
                vbanks[tt].free = [tav]
            thm = head_c(3)
            P.barrier()

            place[0] = mark2
            lam = sb([128, 4], F32, "lam")
            aq, ak = [pair([128, 512], "aq") for _ in range(2)], [pair([128, 512], "ak") for _ in range(2)]
            p0, p1 = Ring(3, [128, 512], name="p0"), Ring(2, [128, 512], name="p1")
            PT = [pair([128, 1280], "PT")] * 2
            st = sb([128, 16, 4], F32, "st")
            t = op("dve", lambda e: e.tensor_tensor(lam[:, 0:2], cols[:, COLS["lq1"][0]:COLS["lq1"][0] + 2], cols[:, COLS["lk1"][0]:COLS["lk1"][0] + 2], ALU.mult), P.last["dve"])
            b = bank()
            t = mm(b.t[:, 0:2], mat("ones"), lam[:, 0:2], True, True, t, b.free)
            tables("log_exp")
            t = op("act", lambda e, b=b: e.activation(lam[:, 0:2], b.t[:, 0:2], ACT.Exp), t)
            b.free = [t]
            t = op("dve", lambda e: e.tensor_tensor(lam[:, 2:3], lam[:, 1:2], lam[:, 0:1], ALU.subtract), t)
            tl = op("dve", lambda e: e.tensor_scalar(lam[:, 3:4], lam[:, 2:3], 1.0, -(0.8 - 0.6 * 1.0), ALU.mult, ALU.add), t)
            qk2, ptf, ptt = {}, [[], []], {}
            qkf = [[], []]

            def prepare2(hd, step):
                k = hd % 2
                if step < 2:
                    proj[step] = dense([(0, wcols("w_in_2", (2056, 2568)[step] + hd * 128, 128))], 8, h)
                if step > 0:
                    name, dst, scale = (("q_norm", aq, 0.125), ("k_norm", ak, 1.0))[step - 1]
                    b, t = proj[step - 1]
                    qk2.setdefault(hd, []).append(chunk_norm(b, t, mat("blk64"), col(name), (dst[k][0][:, :], dst[k][1][:, :]), scale=scale, before=qkf[k]))

            proj = {}
            ready = {}

            def first(n):
                hd, i = n // 4, n % 4
                k, W = hd % 2, 128 * (i + 1)
                ps = []
                for c in range(2):
                    po = 64 * c
                    b = bank()
                    mm3(b.t[:, 0:W], [x[po:po + 64, 128 * i:128 * i + 128] for x in aq[k]], [x[po:po + 64, 0:W] for x in ak[k]],
                        True, False, qk2[hd], b.free)
                    t = mm(b.t[:, 128 * i:W], rident[:, :], rdm[:, :], False, True, t_const[0])
                    p, f, _ = (p0, p1)[c].get()
                    t1 = op("dve", lambda e, b=b, c=c: e.tensor_reduce(st[:, n, c:c + 1], b.t[:, 0:W], AX.X, ALU.max, negate=True), t)
                    tables("log_exp")
                    t2 = op("act", lambda e, b=b, c=c, p=p: e.activation(p[:, 0:W], b.t[:, 0:W], ACT.Exp, bias=st[:, n, c:c + 1], accum_out=st[:, n, 2 + c:3 + c]), t1, f)
                    b.free = [t2]
                    ps.append((p, t2))
                qkf[k] = [t]
                t3 = op("dve", lambda e: e.reciprocal(st[:, n, 2:4], st[:, n, 2:4]), ps[0][1], ps[1][1])
                t4 = op("dve", lambda e: e.tensor_scalar(st[:, n, 3:4], st[:, n, 3:4], lam[:, 3:4], None, ALU.mult), t3, tl)
                a, bb = ps[0][0], ps[1][0]
                t5 = op("dve", lambda e: e.tensor_scalar(a[:, 0:W], a[:, 0:W], st[:, n, 2:3], None, ALU.mult), t3)
                t6 = op("dve", lambda e: e.scalar_tensor_tensor(a[:, 0:W], bb[:, 0:W], st[:, n, 3:4], a[:, 0:W], ALU.mult, ALU.add), t4, t5)
                p1.free[n % 2] = [t6]
                ready[n] = (a, t6)

            def second(n):
                hd, i = n // 4, n % 4
                a, t = ready.pop(n)
                b = bank()
                for s in range(i + 1):
                    t1 = op("pe", lambda e, s=s, b=b: e.transpose(b.t[:, s * 128:(s + 1) * 128], a[:, s * 128:(s + 1) * 128], mat("ident")), t, b.free)
                p0.free[n % 3] = [t1]
                k = hd % 2
                for s in range(i + 1):
                    o = REG[s][2] + 128 * (i - s)
                    t2 = op("act", lambda e, s=s, b=b, o=o: e.activation(PT[k][0][:, o:o + 128], b.t[:, s * 128:(s + 1) * 128], ACT.Copy), t1, ptf[0])
                for s in range(i + 1):
                    o = REG[s][2] + 128 * (i - s)
                    t3 = op("dve", lambda e, s=s, b=b, o=o: e.tensor_tensor(PT[k][1][:, o:o + 128], b.t[:, s * 128:(s + 1) * 128], PT[k][0][:, o:o + 128].bitcast(F32), ALU.subtract), t2, ptf[0])
                b.free = [t3]
                if i < 3:
                    return

                def values():
                    b2 = bank()
                    for j in range(4):
                        o, N = REG[j][2], 512 - 128 * j
                        t4 = mm3(b2.t[:, 128 * j:512], (av[0][:, j, hd * 128:hd * 128 + 128], av[1][:, j, hd * 128:hd * 128 + 128]),
                                 [x[:, o:o + N] for x in PT[k]], j == 0, j == 3, t3, tav, b2.free)
                    ptf[0] = [t4]
                    y, f, _ = tmp["y"].get()
                    slot = tmp["y"].i
                    ty = op("act", lambda e: e.activation(y[:, :], b2.t[:, :], ACT.Copy), t4, f)
                    b2.free = [ty]
                    later.append(lambda: finish(y, slot, ty))

                def finish(y, slot, ty):
                    r, tr = rms(lambda q: y[:, :], 1, mat("ones"), 128, ty)
                    ty = op("dve", lambda e: e.scalar_tensor_tensor(y[:, :], y[:, :], col("a_norm"), r[:, :], ALU.mult, ALU.mult), tr)
                    tmp["rr"].release(ty)
                    t8 = split(y[:, :], ha[0][:, hd, :], ha[1][:, hd, :], ty, scale=1.0 - (0.8 - 0.6 * 1.0))
                    tmp["y"].free[slot] = [t8]
                    y_done.append(t8)
                later.append(values)

            later, y_done = [], []

            def run_later():
                now = later[:]
                del later[:]
                for f in now:
                    f()

            def add_out(m, part, src, *waits):
                b, t = dense([(0, wcols("w_out_2", m * 128, 128, 4 * part, 4))], 4, src, *waits)
                b.free = [op("dve", lambda e: e.tensor_tensor(xT[:, m, :], b.t[:, :], xT[:, m, :], ALU.add), t)]
                return b.free[0]

            for step in range(3):
                prepare2(0, step)
            for n in range(18):
                if n < 16:
                    if n % 4 < 3 and n // 4 < 3:
                        prepare2(n // 4 + 1, n % 4)
                    first(n)
                for m in [m for m in range(8) if OUT[m] == n]:
                    add_out(m, 0, hm, thm)
                run_later()
                if n >= 2:
                    second(n - 2)
            run_later()
            run_later()
            tha = y_done[-1]
            for m in range(8):
                tx = add_out(m, 1, ha, tha)
                add_square(m, tx)
            P.barrier()
            return tx

        def moe():
            place[0] = mark0
            xt = sb([128, 4, 1024], F32, "xt")
            di = [sb([128, 4], I32, "di") for _ in range(2)]
            ei = sb([128, NX + 1], I32, "ei")
            rt = {k: sb([128, 4], F32, k) for k in ("w1", "w2")}
            mark3 = place[0]
            moe_top = top_end
            more = []
            while moe_top - 4096 >= mark3 + 32768 and len(more) < 12:
                moe_top -= 4096
                more.append(Slot(nc.alloc_sbuf_tensor_at(f"stage_moe{len(more)}", [128, 1024], F32, offset=moe_top)))
                more[-1].after = [P.last[e] for e in ("pe", "act", "dve")]
            stream["stage"] += more
            tmp["y"], tmp["rr"] = Ring(2, [128, 512], name="y"), Ring(1, [128, 512], name="rr")
            hb = [sb([128, 1024], F32, "hb") for _ in range(4)]
            lgT = sb([36, 512], F32, "lgT")
            a32 = sb([128, 4, 32], F32R, "a32r")
            rt |= {k: sb([128] + s, F32, k) for k, s in
                  dict(lg=[4, 36], gm=[4], a4=[4, 4], oh=[4, 4], em=[4, 32], a32=[4, 32], o1=[4, 32], o2=[4, 32],
                       v1=[4], v2=[4], gw=[4], vm=[4], ct=[32], nx=[32], cx=[32], on=[32], ps=[4, 32],
                       dx=[32], d1=[4], d2=[4], le=[NX, 32], ei=[NX + 1]).items()}
            ext = mats[:, MATS.index("extra"), :]
            ths = norm_x("norm2")
            b, t = dense([(0, wcols("w_r", 0, 128))], 8, h, parts_ready=ths)
            t = op("act", lambda e, b=b: e.activation(lgT[:, :], b.t[0:36, :], ACT.Identity, bias=col("b_r")[0:36, :]), t)
            b.free = [t]
            b = bank()
            for tt in range(4):
                t = op("pe", lambda e, tt=tt, b=b: e.transpose(b.t[:, 36 * tt:36 * tt + 36], lgT[:, tt * 128:(tt + 1) * 128], mat("ident")[0:36, 0:36]), t, b.free)
            b.free = [op("dve", lambda e, b=b: e.tensor_copy(rt["lg"][:, :, :], b.t[:, 0:144].rearrange("p (a n) -> p a n", a=4)), t)]
            s_sc = sem("s_sc")
            thb = []
            for tt in range(4):
                for q in range(2):
                    b = bank()
                    for k in range(4):
                        for part in (0, 1):
                            t = mm(b.t[:, k * 128:(k + 1) * 128], h[part][:, 4 * q + k, tt * 128:(tt + 1) * 128], rident[:, :],
                                   part == 0, part == 1, b.free, skip=True)
                    t1 = op("act", lambda e, q=q, tt=tt, b=b: e.activation(hb[tt][:, 512 * q:512 * q + 512], b.t[:, :], ACT.Copy), t)
                    b.free = [t1]
                thb.append(t1)
            for tt in range(4):
                for q in range(2):
                    b = bank()
                    for k in range(4):
                        t = op("pe", lambda e, k=k, q=q, tt=tt, b=b: e.transpose(b.t[:, k * 128:(k + 1) * 128], xT[:, 4 * q + k, tt * 128:(tt + 1) * 128], mat("ident")), b.free)
                    t1 = op("act", lambda e, q=q, tt=tt, b=b: e.activation(xt[:, tt, 512 * q:512 * q + 512], b.t[:, :], ACT.Copy), t)
                    b.free = [t1]
            R = rt

            def v(fn, *w):
                return op("dve", fn, P.last["dve"], *w)

            def bc(ap, shape, axis=2):
                return ap.unsqueeze(axis).broadcast_to(shape)

            G = R["lg"][:, :, 0:4]
            E4 = R["lg"][:, :, 4:36].rearrange("p a (g n) -> p a g n", g=4)
            v(lambda e: e.tensor_reduce(R["gm"][:, :], G, AX.X, ALU.max))
            v(lambda e: e.tensor_tensor(R["oh"][:, :, :], G, bc(R["gm"][:, :], [128, 4, 4]), ALU.is_equal))
            v(lambda e: e.tensor_tensor(R["oh"][:, :, :], R["oh"][:, :, :], bc(ext[:, 32:36], [128, 4, 4], 1), ALU.mult))
            v(lambda e: e.tensor_reduce(R["vm"][:, :], R["oh"][:, :, :], AX.X, ALU.max))
            v(lambda e: e.tensor_tensor(R["oh"][:, :, :], R["oh"][:, :, :], bc(R["vm"][:, :], [128, 4, 4]), ALU.is_equal))
            v(lambda e: e.tensor_scalar(R["oh"][:, :, :], R["oh"][:, :, :], -NEG, NEG, ALU.mult, ALU.add))
            EM = R["em"][:, :, :].rearrange("p a (g n) -> p a g n", g=4)
            for g_ in range(4):
                v(lambda e, g_=g_: e.tensor_tensor(EM[:, :, g_, :], E4[:, :, g_, :], bc(R["oh"][:, :, g_], [128, 4, 8]), ALU.add))
            for o_, v_ in (("o1", "v1"), ("o2", "v2")):
                v(lambda e, v_=v_: e.tensor_reduce(R[v_][:, :], R["em"][:, :, :], AX.X, ALU.max))
                v(lambda e, v_=v_: e.tensor_tensor(R["a32"][:, :, :], R["em"][:, :, :], bc(R[v_][:, :], [128, 4, 32]), ALU.is_equal))
                v(lambda e: e.tensor_tensor(R["a32"][:, :, :], R["a32"][:, :, :], bc(ext[:, 36:68], [128, 4, 32], 1), ALU.mult))
                v(lambda e: e.tensor_reduce(R["vm"][:, :], R["a32"][:, :, :], AX.X, ALU.max))
                v(lambda e, o_=o_: e.tensor_tensor(R[o_][:, :, :], R["a32"][:, :, :], bc(R["vm"][:, :], [128, 4, 32]), ALU.is_equal))
                if o_ == "o1":
                    v(lambda e: e.scalar_tensor_tensor(R["em"][:, :, :], R["o1"][:, :, :], 2 * NEG, R["em"][:, :, :], ALU.mult, ALU.add))
            ta = v(lambda e: e.tensor_tensor(a32[:, :, :], R["o1"][:, :, :], R["o2"][:, :, :], ALU.add))
            b, b2 = bank(), bank()
            for tt in range(4):
                for t2_ in range(tt + 1):
                    t = mm(b.t[:, 32 * tt:32 * tt + 32], rmats[:, 5, :] if t2_ == tt else rones[:, :], a32[:, t2_, :], t2_ == 0, t2_ == tt, ta, b.free, skip=True)
                t = mm(b2.t[:, 0:32], rones[:, :], a32[:, tt, :], tt == 0, tt == 3, b2.free)
            v(lambda e, b=b: e.tensor_copy(R["ps"][:, :, :].rearrange("p a n -> p (a n)"), b.t[:, 0:128]), t)
            b.free = [P.last["dve"]]
            v(lambda e, b=b2: e.tensor_copy(R["ct"][:, :], b.t[:, 0:32]))
            b2.free = [P.last["dve"]]
            v(lambda e: e.tensor_scalar(R["nx"][:, :], R["ct"][:, :], float(BLK), None, ALU.is_gt))
            for c in range(2 * BLK, 512, BLK):
                v(lambda e, c=float(c): e.scalar_tensor_tensor(R["nx"][:, :], R["ct"][:, :], c, R["nx"][:, :], ALU.is_gt, ALU.add))
            v(lambda e: e.memset(R["on"][:, :], 1.0))
            v(lambda e: e.tensor_tensor_scan(R["cx"][:, :], R["on"][:, :], R["nx"][:, :], 0.0, ALU.mult, ALU.add))
            v(lambda e: e.tensor_tensor(R["dx"][:, :], R["cx"][:, :], R["nx"][:, :], ALU.subtract))
            v(lambda e: e.tensor_scalar(R["dx"][:, :], R["dx"][:, :], float(BLK), float(BLK * (NB - 1)), ALU.mult, ALU.add))
            v(lambda e: e.tensor_tensor(R["dx"][:, :], R["dx"][:, :], ext[:, 0:32], ALU.subtract))
            v(lambda e: e.tensor_scalar(R["a32"][:, :, :], R["ps"][:, :, :], float(BLK), None, ALU.is_ge))
            v(lambda e: e.tensor_tensor(R["a32"][:, :, :], R["a32"][:, :, :], bc(R["dx"][:, :], [128, 4, 32], 1), ALU.mult))
            v(lambda e: e.tensor_tensor(R["ps"][:, :, :], R["ps"][:, :, :], R["a32"][:, :, :], ALU.add))
            v(lambda e: e.tensor_tensor(R["ps"][:, :, :], R["ps"][:, :, :], bc(ext[:, 0:32], [128, 4, 32], 1), ALU.add))
            for q, o_ in enumerate(("o1", "o2")):
                v(lambda e, o_=o_: e.tensor_tensor(R["a32"][:, :, :], R["ps"][:, :, :], R[o_][:, :, :], ALU.mult))
                v(lambda e: e.tensor_reduce(R["d1"][:, :], R["a32"][:, :, :], AX.X, ALU.add))
                v(lambda e, q=q: e.tensor_copy(di[q][:, :], R["d1"][:, :]))
            tdi = P.last["dve"]
            v(lambda e: e.tensor_tensor(R["le"][:, :, :], bc(R["cx"][:, :], [128, NX, 32], 1), bc(ext[:, 68:68 + NX], [128, NX, 32]), ALU.is_le))
            v(lambda e: e.tensor_reduce(R["ei"][:, 0:NX], R["le"][:, :, :], AX.X, ALU.add))
            v(lambda e: e.tensor_copy(R["ei"][:, NX:NX + 1], R["cx"][:, 31:32]))
            v(lambda e: e.tensor_scalar(R["ei"][:, 0:NX], R["ei"][:, 0:NX], 31.0, None, ALU.min))
            v(lambda e: e.tensor_copy(ei[:, :], R["ei"][:, :]))
            v(lambda e: e.tensor_tensor(R["a4"][:, :, :], G, bc(R["gm"][:, :], [128, 4, 4]), ALU.subtract))
            tables("log_exp")
            tt1 = op("act", lambda e: e.activation(R["a4"][:, :, :], R["a4"][:, :, :], ACT.Exp), P.last["dve"])
            v(lambda e: e.tensor_reduce(R["gw"][:, :], R["a4"][:, :, :], AX.X, ALU.add), tt1)
            v(lambda e: e.reciprocal(R["gw"][:, :], R["gw"][:, :]))
            v(lambda e: e.tensor_tensor(R["v2"][:, :], R["v2"][:, :], R["v1"][:, :], ALU.subtract))
            tables("log_exp")
            tt1 = op("act", lambda e: e.activation(R["v2"][:, :], R["v2"][:, :], ACT.Exp), P.last["dve"])
            v(lambda e: e.tensor_scalar(R["w1"][:, :], R["v2"][:, :], 1.0, None, ALU.add), tt1)
            v(lambda e: e.reciprocal(R["w1"][:, :], R["w1"][:, :]))
            v(lambda e: e.tensor_tensor(R["w1"][:, :], R["w1"][:, :], R["gw"][:, :], ALU.mult))
            v(lambda e: e.tensor_tensor(R["w2"][:, :], R["w1"][:, :], R["v2"][:, :], ALU.mult))

            for tt in range(4):
                for q in range(2):
                    tsc = dma("pool", lambda e, tt=tt, q=q: e.indirect_dma_start(
                        out=xb_d[:, :], out_offset=bass.IndirectOffsetOnAxis(ap=di[q][:, tt:tt + 1], axis=0),
                        in_=hb[tt][:, :], in_offset=None).then_inc(s_sc, 16), s_sc, tdi, thb[tt], t_zero[-1])
            place[0] = x_place
            NGR = 3
            xg = [sb([128, 1024], F32, "xg") for _ in range(NGR)]
            s_xg = [sem("s_xg") for _ in range(NGR)]
            xgT = [pair([128, 8, 128], "xgT") for _ in range(2)]
            hid = [sb([128, 512], F32, "hid") for _ in range(2)]
            hT = [pair([128, 4, 128], "hT") for _ in range(2)]
            yo = [sb([128, 1024], F32, "yo") for _ in range(2)]
            assert place[0] <= x_place + 49152
            s_yo = [sem("s_yo") for _ in range(2)]
            for a in [x for p in xgT + hT for x in p]:
                op("dve", lambda e, a=a: e.memset(a[:, :, BLK:].bitcast(F32), 0.0), P.last["pe"], P.last["act"])
            P.barrier(also=[tsc])

            place[0] = mark3
            for k in range(3):
                stream["split"].append(Slot(*pair([128, 1024], "w_moe")))
                stream["split"][-1].after = [P.last[e] for e in ("pe", "act", "dve")] + [tsc]
            stream["ahead"] = 4
            F = dict(xg=[[] for _ in range(NGR)], xgT=[[], []], hid=[[], []], hT=[[], []], yo=[[], []])
            xg_t, xT_t, hid_t = {}, {}, {}

            def fetch(n, *waits):
                k = n % NGR
                xg_t[n] = dma("pool", lambda e: e.dma_start(xg[k][0:BLK, :], xb_d[n * BLK:(n + 1) * BLK, :]).then_inc(s_xg[k], 16), s_xg[k], F["xg"][k], *waits)

            def turn_x(n):
                k = n % NGR
                for q in range(2):
                    b = bank()
                    for j in range(4):
                        t = op("pe", lambda e, j=j, q=q, b=b: e.transpose(b.t[:, j * BLK:(j + 1) * BLK], xg[k][0:BLK, (4 * q + j) * 128:(4 * q + j + 1) * 128], mat("ident")[0:BLK, 0:BLK]), xg_t[n], b.free)
                    t1 = split(b.t[:, 0:4 * BLK].rearrange("p (k n) -> p k n", k=4), xgT[n % 2][0][:, 4 * q:4 * q + 4, 0:BLK], xgT[n % 2][1][:, 4 * q:4 * q + 4, 0:BLK], t, F["xgT"][n % 2])
                    b.free = [t1]
                F["xg"][k] = [t]
                xT_t[n] = t1

            def gate_up(n, wsrc, ahead=True):
                x = xgT[n % 2]
                bs = []
                for name in ("w_gate_2", "w_up_2"):
                    b = bank()
                    for kk in range(4):
                        u = use([(0, wsrc(name, 2 * kk, 2))], 2, 512, ahead=ahead)
                        for j in range(2):
                            t = mm3(b.t[:, :], [y[:, 2 * kk + j, :] for y in x], (u.H[:, j, :], u.L[:, j, :]),
                                    kk == 0 and j == 0, kk == 3 and j == 1, u.t_lo, u.t_hi, b.free, xT_t[n])
                        u.done = t
                    bs.append((b, t))
                F["xgT"][n % 2] = [t]
                hd_ = hid[n % 2]
                (bg, tg_), (bu, tu_) = bs
                tables("silu")
                t1 = op("act", lambda e: e.activation(hd_[0:BLK, :], bg.t[0:BLK, :], ACT.Silu), tg_, F["hid"][n % 2])
                bg.free = [t1]
                t2 = op("dve", lambda e: e.tensor_tensor(hd_[0:BLK, :], hd_[0:BLK, :], bu.t[0:BLK, :], ALU.mult), t1, tu_)
                bu.free = [t2]
                hid_t[n] = t2

            def down(n, wsrc, ahead=True):
                hd_, t2 = hid[n % 2], hid_t.pop(n)
                b = bank()
                for j in range(4):
                    t3 = op("pe", lambda e, j=j, b=b: e.transpose(b.t[:, j * BLK:(j + 1) * BLK], hd_[0:BLK, j * 128:(j + 1) * 128], mat("ident")[0:BLK, 0:BLK]), t2, b.free)
                F["hid"][n % 2] = [t3]
                hh = hT[n % 2]
                t4 = split(b.t[:, 0:4 * BLK].rearrange("p (k n) -> p k n", k=4), hh[0][:, :, 0:BLK], hh[1][:, :, 0:BLK], t3, F["hT"][n % 2])
                b.free = [t4]
                ob = [bank(), bank()]
                for j in range(4):
                    u = use([(0, wsrc("w_down_2", j, 1))], 1, 1024, ahead=ahead)
                    for c in range(2):
                        t = mm3(ob[c].t[:, :], (hh[0][:, j, :], hh[1][:, j, :]), (u.H[:, 0, 512 * c:512 * c + 512], u.L[:, 0, 512 * c:512 * c + 512]),
                                j == 0, j == 3, u.t_lo, u.t_hi, ob[c].free, t4)
                    u.done = t
                F["hT"][n % 2] = [t]
                o = yo[n % 2]
                t1 = op("act", lambda e: e.activation(o[0:BLK, 0:512], ob[0].t[0:BLK, :], ACT.Copy), t, F["yo"][n % 2])
                t2 = op("act", lambda e: e.activation(o[0:BLK, 512:1024], ob[1].t[0:BLK, :], ACT.Copy))
                ob[0].free, ob[1].free = [t1], [t2]
                k = n % 2
                ts = dma("pool", lambda e: e.dma_start(yb_d[n * BLK:(n + 1) * BLK, :], o[0:BLK, :]).then_inc(s_yo[k], 16), s_yo[k], t1, t2)
                F["yo"][k] = [ts]
                return ts

            for n in range(NGR):
                fetch(n)
            turn_x(0)
            turn_x(1)

            def wof(n):
                return lambda name, k, c: A[name][n].rearrange("(k p) n -> p k n", p=128)[:, k:k + c, :]
            gate_up(0, wof(0))
            for n in range(NB):
                if n + 1 < NB:
                    gate_up(n + 1, wof(n + 1))
                if n + 2 < NB:
                    turn_x(n + 2)
                if n + NGR < NB:
                    fetch(n + NGR)
                down(n, wof(n))
            stores = [F["yo"][0], F["yo"][1]]
            P.barrier(engs=("pe", "act", "dve", "pool", "sp"), also=stores[0] + stores[1])

            for x in range(NX):
                P.region_begin()
                F.update(xg=[[] for _ in range(NGR)], xgT=[[], []], hid=[[], []], hT=[[], []], yo=[[], []])
                for bb in banks:
                    bb.free = []
                for uu in units:
                    uu.t_lo = uu.t_hi = uu.done = None
                del holes[len(units):]
                n = NB + x
                fetch(n)
                turn_x(n)

                def wdyn(name, k, c, x=x):
                    def src(e):
                        r = P.regs[x]
                        w = A[name].rearrange("e (k p) n -> e p k n", p=128)
                        return w[bass.ds(r, 1), :, k:k + c, :].rearrange("e p k n -> (e p) k n")
                    return src
                gate_up(n, wdyn, ahead=False)
                ts = down(n, wdyn, ahead=False)
                P.barrier(also=[ts], engs=("pe", "act", "dve", "pool", "sp"))
                P.region_end(x)

            place[0] = x_place
            yy = [[sb([128, 1024], F32, "yy") for _ in range(2)] for _ in range(4)]
            s_out = sem("s_out")
            t_g = [[], [], [], []]
            for tt in range(4):
                for q in range(2):
                    s = sem("s_g")
                    t_g[tt].append(dma("pool", lambda e, tt=tt, q=q, s=s: e.indirect_dma_start(
                        out=yy[tt][q][:, :], out_offset=None, in_=yb_d[:, :],
                        in_offset=bass.IndirectOffsetOnAxis(ap=di[q][:, tt:tt + 1], axis=0)).then_inc(s, 16), s))
            for tt in range(4):
                t1 = None
                for q, w in enumerate(("w1", "w2")):
                    t1 = op("dve", lambda e, q=q, w=w, tt=tt: e.scalar_tensor_tensor(xt[:, tt, :], yy[tt][q][:, :], R[w][:, tt:tt + 1], xt[:, tt, :], ALU.mult, ALU.add), t1, t_g[tt][q])
                tend = dma("act", lambda e, tt=tt: e.dma_start(out[tt * 128:(tt + 1) * 128, :], xt[:, tt, :]).then_inc(s_out, 16), s_out, t1)
            P.q["act"].append([None, [tend], None])
            P.ei = ei


        h = (hH, hL)
        for k in range(8):
            add_square(k, t_x[k])
        hold_ahead()
        tx = ffn("w1_gate", "w1_up", "w1_down", "g_ffn1")
        tx = mixer1()
        tx = ffn("w2_gate", "w2_up", "w2_down", "g_ffn2")
        tx = mixer2()
        moe()
        block = ctx.enter_context(nc.Block())
        P.emit(block)


def _layout(inputs):
    f = {k: np.asarray(v) for k, v in inputs.items()}

    def chunks(v):
        return v.reshape(-1, 128).T

    def twice(v):
        return np.concatenate([v.reshape(-1), v.reshape(-1)])[:, None]

    def padded(v, n=128):
        v = v.reshape(-1)
        return np.concatenate([v, np.zeros(n - v.size, np.float32)])[:, None]

    inv = (np.float32(10000.0) ** (-np.arange(0, 64, 2, dtype=np.float32) / np.float32(64))).astype(np.float32)
    p = {
        "g_ffn1": chunks(f["g_ffn1"]), "g_mix": chunks(f["g_mix"]), "g_cq": chunks(f["g_cq"]),
        "g_q_a": twice(f["g_q_a"]), "g_k_a": twice(f["g_k_a"]), "g_ffn2": chunks(f["g_ffn2"]),
        "norm1": chunks(f["norm1_w_2"]), "conv_w": np.concatenate([chunks(f["conv_w_2"][0, j]) for j in range(4)], axis=1),
        "conv_b": chunks(f["conv_b_2"]), "m_norm": chunks(f["m_norm_w_2"]), "q_norm": twice(f["q_norm_w_2"]),
        "k_norm": twice(f["k_norm_w_2"]), "a_norm": chunks(f["a_norm_w_2"]), "bi": padded(f["b_igate_2"]),
        "bf": padded(f["b_fgate_2"]), "lq1": padded(f["lambda_q1_2"]), "lq2": padded(f["lambda_q2_2"]),
        "lk1": padded(f["lambda_k1_2"]), "lk2": padded(f["lambda_k2_2"]),
        "norm2": chunks(f["norm2_w_2"]), "b_r": padded(np.concatenate([f["b_group_2"][0], f["b_expert_2"][0]])),
        "inv_freq": np.tile(inv, 4)[:, None], "sgn": np.tile(np.repeat(np.array([-1.0, 1.0], np.float32), 32), 2)[:, None],
        "eps": np.full((128, 1), EPS, np.float32), "one": np.ones((128, 1), np.float32),
    }
    a = {"cols": np.concatenate([p[k].reshape(128, -1) for k in COLS], axis=1), "mats": shape_constants()}
    a["x"] = f["x"][0].T.reshape(8, 128, 512).transpose(1, 0, 2)
    a["positions"] = f["positions"]
    w, w2 = f["w_in"][0], f["w_in_2"][0]
    for k in ("w1_gate", "w1_up", "w1_down", "w2_gate", "w2_up", "w2_down", "w_in", "w_o_a", "w_o_b", "w_out", "w_uq_a",
              "w_q_idx", "w_uv_a", "w_in_2", "w_out_2", "w_gate_2", "w_up_2", "w_down_2"):
        a[k] = f[k][0]
    a["w_k2"] = np.concatenate([w[:, 256:320], w[:, 256:320], w[:, 448:512], w[:, 448:512]], axis=1)
    a["w_vw"] = np.concatenate([w[:, 320:448], w[:, 512:520]], axis=1)
    gap = np.zeros((1024, 28), np.float32)
    a["w_if"] = np.concatenate([w2[:, 2048:2052], gap, w2[:, 2052:2056], gap, gap, gap, gap[:, 0:8]], axis=1)
    a["w_r"] = np.concatenate([f["w_group_2"][0], f["w_expert_2"][0], np.zeros((1024, 92), np.float32)], axis=1)
    return {k: np.ascontiguousarray(v) for k, v in a.items()}


def kernel(**inputs):
    import numpy as _np
    import concourse.bacc as _bacc
    from concourse import mybir as _mybir
    from concourse.bass_utils import run_bass_kernel_spmd as _run

    nc = _bacc.Bacc("TRN2", target_bir_lowering=False, num_devices=1)
    arrays = _layout(inputs)
    handles = {k: nc.dram_tensor(k, v.shape, _mybir.dt.from_np(v.dtype), kind="ExternalInput").ap() for k, v in arrays.items()}
    out = nc.dram_tensor("out", (512, 1024), _mybir.dt.float32, kind="ExternalOutput").ap()
    build(nc, handles, out)
    r = _run(nc, [arrays], core_ids=[0])
    return _np.asarray(r.results[0]["out"]).reshape(1, 512, 1024)
```
